# Optimizing a Trainium2 kernel written in Bass

```python
import jax, jax.numpy as jnp
from jax import lax
import numpy as np

D_MODEL = 1024
BATCH = 1
SEQ = 1024
DEPTH = 1
DEC_BATCH = 1
DEC_SEQ = 64
PAST_LEN = 128

CHUNK = 64
N_META = 16
N_HEADS = 4
HEAD_K = 64
HEAD_V = 128
RET_K = N_HEADS * HEAD_K
RET_V = N_HEADS * HEAD_V
GLA_K = N_HEADS * HEAD_K
GLA_V = N_HEADS * HEAD_V
GLA_RANK = 16
GATE_NORM = 16.0
ROPE_BASE = 10000.0
N_GROUPS = 4
EXPERTS_PER_GROUP = 8
N_EXPERTS = N_GROUPS * EXPERTS_PER_GROUP
TOP_K_INNER = 2
D_EXPERT = 512
MOE_BLOCK = 128
NORM_EPS = 1e-6
PROJ_SIZES = (RET_K, RET_K, RET_V, RET_V, GLA_K, GLA_K, GLA_V, GLA_V, GLA_RANK, D_MODEL, D_MODEL)
D_PROJ = 2 * (2 * RET_K + 2 * RET_V) + GLA_RANK + 2 * D_MODEL

kernel_name = "hybrid_retention_gla_hiermoe_stream_step"

def _rmsnorm(x, g):
    xf = x.astype(jnp.float32)
    y = xf * lax.rsqrt(jnp.mean(xf * xf, axis=-1, keepdims=True) + NORM_EPS)
    return (y * g.astype(jnp.float32)).astype(x.dtype)

def _rotary(x, pos):
    half = HEAD_K // 2
    inv = ROPE_BASE ** (-2.0 * jnp.arange(half, dtype=jnp.float32) / HEAD_K)
    ang = pos[..., None] * inv
    cos = jnp.cos(ang)[None, :, :, None, :]
    sin = jnp.sin(ang)[None, :, :, None, :]
    x1, x2 = x[..., :half], x[..., half:]
    return jnp.concatenate([x1 * cos - x2 * sin, x1 * sin + x2 * cos], axis=-1)

def _retention(q, k, v, g, pos, s0):
    B, NC, L = q.shape[:3]
    q = _rotary(q, pos)
    k = _rotary(k, pos) * (HEAD_K ** -0.5)
    log_g = jnp.log1p(-jnp.exp2(-5.0 - jnp.arange(N_HEADS, dtype=jnp.float32)))
    idx = jnp.arange(L, dtype=jnp.float32)
    dmat = jnp.exp(jnp.abs(idx[:, None] - idx[None, :])[None] * log_g[:, None, None])
    scores = jnp.einsum("bclhk,bcmhk->bchlm", q, k) * dmat
    intra = jnp.einsum("bchlm,bcmhv->bclhv", scores, v)
    k_dec = jnp.exp((L - 1.0 - idx)[:, None] * log_g)[:, :, None]
    u = jnp.einsum("bclhk,bclhv->bchkv", k * k_dec, v)
    c_dec = jnp.exp(L * log_g)[:, None, None]

    def step(s, u_c):
        return s * c_dec + u_c, s

    s_last, s_prev = lax.scan(step, s0, jnp.moveaxis(u, 1, 0))
    q_dec = jnp.exp((idx + 1.0)[:, None] * log_g)[:, :, None]
    inter = jnp.einsum("bclhk,cbhkv->bclhv", q * q_dec, s_prev)
    o = intra + inter
    mu = jnp.mean(o, axis=-1, keepdims=True)
    var = jnp.mean(jnp.square(o - mu), axis=-1, keepdims=True)
    o = (o - mu) * lax.rsqrt(var + NORM_EPS)
    return o.reshape(B, NC, L, RET_V) * jax.nn.silu(g), s_last

def _gla(q, k, v, g, gate_logits, s0, g_norm):
    B, NC, L = q.shape[:3]
    q = q * (HEAD_K ** -0.5)
    log_a = jax.nn.log_sigmoid(gate_logits) / GATE_NORM
    b = jnp.cumsum(log_a, axis=2)
    b_last = b[:, :, -1]
    u = jnp.einsum("bclhk,bclhv->bchkv", k * jnp.exp(b_last[:, :, None] - b), v)
    a = jnp.exp(b_last)[..., None]

    def step(s, inp):
        a_c, u_c = inp
        s = a_c * s + u_c
        return s, s

    s_last, s_all = lax.scan(step, s0, (jnp.moveaxis(a, 1, 0), jnp.moveaxis(u, 1, 0)))
    o = jnp.einsum("bclhk,cbhkv->bclhv", q, s_all)
    o = o * lax.rsqrt(jnp.mean(o * o, axis=-1, keepdims=True) + NORM_EPS) * g_norm.astype(jnp.float32)
    return o.reshape(B, NC, L, GLA_V) * jax.nn.silu(g), s_last

def _token_mixer(h, pos, s_ret, s_gla, w_in, w_gla_gk2, b_gla_gk, g_gla_norm, w_br_ret, w_br_gla, w_out):
    B, NC, L, _ = h.shape
    f32 = jnp.float32
    proj = (h @ w_in).astype(f32)
    rq, rk, rv, rg, gq, gk, gv, gg, glr, z_ret, z_gla = jnp.split(
        proj, [int(c) for c in np.cumsum(PROJ_SIZES)[:-1]], axis=-1)
    heads = lambda t, d: t.reshape(B, NC, L, N_HEADS, d)
    o_ret, s_ret_new = _retention(heads(rq, HEAD_K), heads(rk, HEAD_K), heads(rv, HEAD_V), rg,
                                  pos, s_ret.astype(f32))
    gate_logits = glr @ w_gla_gk2.astype(f32) + b_gla_gk.astype(f32)
    o_gla, s_gla_new = _gla(heads(gq, HEAD_K), heads(gk, HEAD_K), heads(gv, HEAD_V), gg,
                            heads(gate_logits, HEAD_K), s_gla.astype(f32), g_gla_norm)
    merged = jax.nn.sigmoid(z_ret) * (o_ret @ w_br_ret) + jax.nn.sigmoid(z_gla) * (o_gla @ w_br_gla)
    y = merged.astype(h.dtype) @ w_out
    return y.astype(h.dtype), s_ret_new, s_gla_new

def _hier_moe(x, w_rg, b_rg, w_re, b_re, w_gate, w_up, w_down):
    T, D = x.shape
    f32 = jnp.float32
    lg = (x @ w_rg + b_rg).astype(f32)
    grp = jnp.argmax(lg, axis=-1)
    p_grp = jnp.take_along_axis(jax.nn.softmax(lg, axis=-1), grp[:, None], axis=1)[:, 0]
    le = (x @ w_re + b_re).astype(f32).reshape(T, N_GROUPS, EXPERTS_PER_GROUP)
    le_sel = le[jnp.arange(T), grp]
    top_v, top_i = lax.top_k(le_sel, TOP_K_INNER)
    gate = jax.nn.softmax(top_v, axis=-1) * p_grp[:, None]
    eid = (grp[:, None] * EXPERTS_PER_GROUP + top_i).reshape(-1).astype(jnp.int32)
    tok = jnp.repeat(jnp.arange(T, dtype=jnp.int32), TOP_K_INNER)
    wgt = gate.reshape(-1)
    A = T * TOP_K_INNER
    order = jnp.argsort(eid)
    e_s, tok_s, w_s = eid[order], tok[order], wgt[order]
    counts = jnp.bincount(eid, length=N_EXPERTS)
    padded = (counts + MOE_BLOCK - 1) // MOE_BLOCK * MOE_BLOCK
    pad_end = jnp.cumsum(padded)
    pad_start = pad_end - padded
    start = jnp.cumsum(counts) - counts
    dest = pad_start[e_s] + jnp.arange(A, dtype=jnp.int32) - start[e_s]
    n_blocks = -(-A // MOE_BLOCK) + N_EXPERTS
    P = n_blocks * MOE_BLOCK
    buf_tok = jnp.full((P,), T, jnp.int32).at[dest].set(tok_s)
    buf_w = jnp.zeros((P,), f32).at[dest].set(w_s)
    blk_e = jnp.minimum(jnp.searchsorted(pad_end, jnp.arange(n_blocks) * MOE_BLOCK, side="right"),
                        N_EXPERTS - 1)
    x_pad = jnp.concatenate([x, jnp.zeros((1, D), x.dtype)], axis=0)
    xb = x_pad[buf_tok].reshape(n_blocks, MOE_BLOCK, D)

    def run_block(args):
        xb_i, e = args
        hid = jax.nn.silu(xb_i @ w_gate[e]) * (xb_i @ w_up[e])
        return hid @ w_down[e]

    yb = lax.map(run_block, (xb, blk_e))
    y = jnp.zeros((T + 1, D), f32).at[buf_tok].add(yb.reshape(P, D).astype(f32) * buf_w[:, None])
    return y[:T].astype(x.dtype)

def _layer(x, pad, pos, s_ret, s_gla, g_mix, w_in, w_gla_gk2, b_gla_gk, g_gla_norm, w_br_ret,
           w_br_gla, w_out, g_ffn, w_rg, b_rg, w_re, b_re, w_gate, w_up, w_down):
    B, N, D = x.shape
    NC, L = pos.shape
    h = jnp.pad(_rmsnorm(x, g_mix), ((0, 0), (pad, 0), (0, 0))).reshape(B, NC, L, D)
    y, s_ret_new, s_gla_new = _token_mixer(h, pos, s_ret, s_gla, w_in, w_gla_gk2, b_gla_gk,
                                           g_gla_norm, w_br_ret, w_br_gla, w_out)
    x = x + y.reshape(B, NC * L, D)[:, pad:]
    h2 = _rmsnorm(x, g_ffn).reshape(B * N, D)
    x = x + _hier_moe(h2, w_rg, b_rg, w_re, b_re, w_gate, w_up, w_down).reshape(B, N, D)
    return x, s_ret_new, s_gla_new

def setup_inputs(seed: int = 0) -> dict:
    key = jax.random.key(seed)
    ks = jax.random.split(key, 22)
    f32 = jnp.float32
    nrm = lambda k, shape, scale: jax.random.normal(k, shape, f32) * scale
    st = (DEPTH, DEC_BATCH, N_HEADS, HEAD_K, HEAD_V)
    return {
        "x_prompt": nrm(ks[0], (BATCH, SEQ, D_MODEL), 1.0),
        "x_sample": nrm(ks[1], (DEC_BATCH, DEC_SEQ, D_MODEL), 1.0),
        "state_ret": nrm(ks[2], st, 0.5),
        "state_gla": nrm(ks[3], st, 0.5),
        "meta_tokens": nrm(ks[4], (N_META, D_MODEL), 1.0),
        "g_mix": 1.0 + nrm(ks[5], (DEPTH, D_MODEL), 0.01),
        "w_in": nrm(ks[6], (DEPTH, D_MODEL, D_PROJ), D_MODEL ** -0.5),
        "w_gla_gk2": nrm(ks[7], (DEPTH, GLA_RANK, GLA_K), GLA_RANK ** -0.5),
        "b_gla_gk": nrm(ks[8], (DEPTH, GLA_K), 0.1),
        "g_gla_norm": 1.0 + nrm(ks[9], (DEPTH, HEAD_V), 0.01),
        "w_br_ret": nrm(ks[10], (DEPTH, RET_V, D_MODEL), RET_V ** -0.5),
        "w_br_gla": nrm(ks[11], (DEPTH, GLA_V, D_MODEL), GLA_V ** -0.5),
        "w_out": nrm(ks[12], (DEPTH, D_MODEL, D_MODEL), D_MODEL ** -0.5),
        "g_ffn": 1.0 + nrm(ks[13], (DEPTH, D_MODEL), 0.01),
        "w_router_group": nrm(ks[14], (DEPTH, D_MODEL, N_GROUPS), D_MODEL ** -0.5),
        "b_router_group": nrm(ks[15], (DEPTH, N_GROUPS), 0.01),
        "w_router_expert": nrm(ks[16], (DEPTH, D_MODEL, N_EXPERTS), D_MODEL ** -0.5),
        "b_router_expert": nrm(ks[17], (DEPTH, N_EXPERTS), 0.01),
        "w_exp_gate": nrm(ks[18], (DEPTH, N_EXPERTS, D_MODEL, D_EXPERT), D_MODEL ** -0.5),
        "w_exp_up": nrm(ks[19], (DEPTH, N_EXPERTS, D_MODEL, D_EXPERT), D_MODEL ** -0.5),
        "w_exp_down": nrm(ks[20], (DEPTH, N_EXPERTS, D_EXPERT, D_MODEL), D_EXPERT ** -0.5),
        "g_final": 1.0 + nrm(ks[21], (D_MODEL,), 0.01),
    }

def reference(x_prompt, x_sample, state_ret, state_gla, meta_tokens, g_mix, w_in, w_gla_gk2, b_gla_gk,
              g_gla_norm, w_br_ret, w_br_gla, w_out, g_ffn, w_router_group, b_router_group,
              w_router_expert, b_router_expert, w_exp_gate, w_exp_up, w_exp_down, g_final):
    f32 = jnp.float32
    B, S, D = x_prompt.shape
    Ts = x_sample.shape[1]
    xp = jnp.concatenate([jnp.broadcast_to(meta_tokens.astype(x_prompt.dtype)[None], (B, N_META, D)),
                          x_prompt], axis=1)
    pad_p = CHUNK - N_META
    pos_p = (jnp.arange(CHUNK + S, dtype=f32) - CHUNK).reshape(-1, CHUNK)
    pos_s = (PAST_LEN + jnp.arange(Ts, dtype=f32)).reshape(1, Ts)
    zero_state = jnp.zeros((B, N_HEADS, HEAD_K, HEAD_V), f32)
    xs = x_sample
    ret_p, gla_p, ret_s, gla_s = [], [], [], []
    for l in range(DEPTH):
        lw = (g_mix[l], w_in[l], w_gla_gk2[l], b_gla_gk[l], g_gla_norm[l], w_br_ret[l], w_br_gla[l],
              w_out[l], g_ffn[l], w_router_group[l], b_router_group[l], w_router_expert[l],
              b_router_expert[l], w_exp_gate[l], w_exp_up[l], w_exp_down[l])
        xp, sr, sg = _layer(xp, pad_p, pos_p, zero_state, zero_state, *lw)
        ret_p.append(sr.astype(x_prompt.dtype))
        gla_p.append(sg.astype(x_prompt.dtype))
        xs, sr, sg = _layer(xs, 0, pos_s, state_ret[l], state_gla[l], *lw)
        ret_s.append(sr.astype(state_ret.dtype))
        gla_s.append(sg.astype(state_gla.dtype))
    y_prompt = _rmsnorm(xp, g_final)[:, N_META:]
    y_sample = _rmsnorm(xs, g_final)
    return (y_prompt, y_sample, jnp.stack(ret_p), jnp.stack(gla_p), jnp.stack(ret_s), jnp.stack(gla_s))


_drawn_inputs = setup_inputs


def setup_inputs(seed=0):
    import zlib

    import numpy as np

    out = dict(_drawn_inputs(seed))
    spreads = {}
    factors = {'state_gla': 64.0,
     'g_mix': 3.242,
     'g_gla_norm': 6.138,
     'g_ffn': 8.362,
     'b_router_group': 47.153,
     'b_router_expert': 5.828,
     'g_final': 29.98}
    for name, (base, spread) in spreads.items():
        noise = np.random.default_rng([zlib.crc32(name.encode()), seed]).standard_normal(out[name].shape)
        drawn = base * np.exp(spread * noise) if base else spread * noise
        out[name] = __import__('jax').numpy.asarray(drawn.astype(out[name].dtype))
    for name, factor in factors.items():
        out[name] = (out[name] * factor).astype(out[name].dtype)
    return out
```

```python
from contextlib import ExitStack

import numpy as np

import concourse.bass as bass
from concourse import mybir

ALU = mybir.AluOpType
ACT = mybir.ActivationFunctionType
AX = mybir.AxisListType
F32 = mybir.dt.float32
F32R = mybir.dt.float32r
I32 = mybir.dt.int32
U32 = mybir.dt.uint32

P = 128
D = 1024
DC = D // P
CHUNK = 64
N_META = 16
SEQ = 1024
DEC_SEQ = 64
PAST_LEN = 128
HEADS = 4
HK = 64
HV = 128
RANK = 16
ROPE_BASE = 10000.0
EPS = 1e-6

ROWS = DEC_SEQ + CHUNK + SEQ
FIRST_META = DEC_SEQ + CHUNK - N_META
TILES = ROWS // P
TPS = 3
SUPER = TILES // TPS
TOK = TPS * P
NHB = 2 * HEADS
HW = 2 * HK + 2 * HV
ITEMS = NHB * TPS
RET_ITEMS = HEADS * TPS

PIECE = 1024
OUT_COLS = [(0, 384), (384, 384), (768, 256)]
PIECES = [1] + [3] * NHB + [3] * DC + [3, 3, 2]
BLOCKS = len(PIECES)
PIECE0 = [sum(PIECES[:w]) for w in range(BLOCKS)]
NP_SB = sum(PIECES)
STAGE = 3
W_HEAD, W_Z, W_OUT = 1, 1 + NHB, 1 + NHB + DC

GROUPS = 4
PER_GROUP = 8
EXPERTS = GROUPS * PER_GROUP
DE = 512
EC = DE // P
TB = 96
PAIRS = 2 * (N_META + SEQ + DEC_SEQ)
MAX_BLOCKS = PAIRS // TB + EXPERTS
MAX_PER_EXPERT = -(-(PAIRS // 2) // TB)
LIST = (MAX_BLOCKS + 1) * TB
DUMP = LIST
EP = 6
EPC = 2048
BIG = 1e30

SEED = 4

C_IDENT, C_DMAT, C_TRI, C_LOW = 0, 128, 128 + HEADS * 128, 256 + HEADS * 128
C_KDEC = C_LOW + 128
C_QDEC = C_KDEC + 2 * HEADS
C_IND = C_QDEC + HEADS
C_VALID = C_IND + 2
C_DUMP = C_VALID + TILES
C_TOKID = C_DUMP + 2 * TILES
C_IOTA = C_TOKID + 4 * TILES
C_GRP = C_IOTA + EXPERTS
C_STEP = C_GRP + EXPERTS
C_TRI32 = C_STEP + MAX_PER_EXPERT
C_TRI32I = C_TRI32 + EXPERTS
C_IOTAB = C_TRI32I + EXPERTS
C_ROT = C_IOTAB + 64
ROT = 3 * (HK // 2)
C_END = C_ROT + TILES * ROT


def shape_constants():
    c = np.zeros((P, C_END), np.float32)
    r = np.arange(P)
    same = (r[:, None] // CHUNK) == (r[None, :] // CHUNK)
    c[:, C_IDENT:C_IDENT + P] = np.eye(P)
    log_g = np.log1p(-np.exp2(-5.0 - np.arange(HEADS)))
    idx = r % CHUNK
    for h in range(HEADS):
        c[:, C_DMAT + h * P:C_DMAT + (h + 1) * P] = np.where(
            same, np.exp(np.abs(idx[:, None] - idx[None, :]) * log_g[h]), 0) * HK ** -0.5
        for k in range(2):
            c[:, C_KDEC + k * HEADS + h] = np.exp((CHUNK - 1.0 - idx) * log_g[h]) * HK ** -0.5 * (r // CHUNK == k)
        c[:, C_QDEC + h] = np.exp((idx + 1.0) * log_g[h])
    c[:, C_TRI:C_TRI + P] = same & (r[:, None] > r[None, :])
    c[:, C_LOW:C_LOW + P] = r[:, None] < r[None, :]
    c[:CHUNK, C_IND] = 1
    c[CHUNK:, C_IND + 1] = 1
    row = np.arange(TILES)[None, :] * P + r[:, None]
    valid = (row < DEC_SEQ) | (row >= FIRST_META)
    c[:, C_VALID:C_VALID + TILES] = valid
    for k in range(2):
        c[:, C_DUMP + k * TILES:C_DUMP + (k + 1) * TILES] = np.where(valid, 0, DUMP + 2 * r[:, None] + k)
    pair = 2 * row[:, :, None] + np.arange(2)
    c[:, C_TOKID:C_TOKID + 4 * TILES] = np.stack([pair // 2, pair], axis=-1).reshape(P, -1)
    c[:, C_IOTA:C_IOTA + EXPERTS] = np.arange(EXPERTS)
    c[:, C_GRP:C_GRP + EXPERTS] = np.arange(EXPERTS) // PER_GROUP
    c[:, C_STEP:C_STEP + MAX_PER_EXPERT] = np.arange(MAX_PER_EXPERT) * TB
    e = np.arange(EXPERTS)
    c[:EXPERTS, C_TRI32:C_TRI32 + EXPERTS] = (e[:, None] < e[None, :]) * float(TB)
    c[:EXPERTS, C_TRI32I:C_TRI32I + EXPERTS] = e[:, None] <= e[None, :]
    c[:, C_IOTAB:C_IOTAB + 64] = np.arange(64)
    pos = np.where(row < DEC_SEQ, PAST_LEN + row, row - DEC_SEQ - CHUNK).astype(np.float32)
    inv = (ROPE_BASE ** (-2.0 * np.arange(HK // 2) / HK)).astype(np.float32)
    ang = (pos[:, :, None] * inv).astype(np.float64)
    rot = np.concatenate([np.cos(ang), -np.sin(ang), np.sin(ang)], axis=-1)
    c[:, C_ROT:] = rot.reshape(P, TILES * ROT)
    return c


def empty_list():
    s = np.zeros((LIST + 2 * P, 2), np.int32)
    s[:, 1] = 2 * ROWS + np.arange(LIST + 2 * P) % TB
    return s


def build(nc, x_all, states, consts, list_init, g_mix, g_ffn, g_final, g_gla, wmix, gk2, w_router, b_router, wexp,
          y_all, raw_out, fin_out):
    x2_dram = nc.dram_tensor("x2_scratch", (TILES, P, D), F32).ap()
    h2_dram = nc.dram_tensor("h2_scratch", (ROWS, D), F32).ap()
    list_dram = nc.dram_tensor("pair_list", (LIST + 2 * P, 2), I32).ap()
    yb_dram = nc.dram_tensor("expert_out", (2 * ROWS + TB, D), F32).ap()

    with ExitStack() as ctx:
        arena = ctx.enter_context(nc.sbuf_tensor("arena", [P, (229344 - 16512) // 4], F32))
        base = 16512
        limit = 229344
        place = [base]

        def at(name, shape, dt=F32):
            size = 4 * int(np.prod(shape[1:]))
            t = nc.alloc_sbuf_tensor_at(name, list(shape), dt, offset=place[0])
            place[0] += -(-size // 32) * 32
            assert place[0] <= limit, (name, place[0])
            return t

        def sem(name):
            return ctx.enter_context(nc.semaphore(name))

        cst = at("cst", [P, C_END])
        logits = at("logits", [P, TILES, 40])
        half = at("half", [P, 4])
        keep_base = place[0]

        hT = [at(f"hT{i}", [P, DC, TOK], F32R) for i in range(2)]
        oT_at = place[0]
        oT = [at(f"oT{i}", [P, NHB, TOK], F32R) for i in range(2)]
        oT_end = place[0]
        mT = [at(f"mT{i}", [P, DC, TOK], F32R) for i in range(2)]
        stage = [at(f"stage{i}", [P, PIECE]) for i in range(STAGE)]
        whl = [[at(f"w{i}{j}", [P, 3 * PIECE], F32R) for j in range(2)] for i in range(2)]
        H = [at(f"H{j}", [P, D]) for j in range(TPS)]
        XR = [at(f"XR{j}", [P, D]) for j in range(TPS)]
        gmix = at("gmix", [P, D])
        gffn = at("gffn", [P, D])
        ggla = at("ggla", [P, HV])
        gk2s = at("gk2s", [RANK + 1, HEADS * HK])
        glrT = at("glrT", [32, TOK])
        wr = at("wr", [P, DC, EXPERTS + GROUPS])
        rb = at("rb", [P, EXPERTS + GROUPS])
        S0 = at("S0", [HK, NHB, HV])
        RAW = at("RAW", [HK, HEADS, HV])
        SW = at("SW", [HK, 4, 2, HV])
        keep = at("keep", [HK, 1])
        pS = at("pS", [P, 4, HW])
        qk = at("qk", [P, 2, 2 * HK])
        rt = at("rt", [P, 2 * HK])
        kd = at("kd", [P, 2, 2, HK])
        qkT = at("qkT", [HK, 4 * P])
        sT = at("sT", [P, P])
        og = at("og", [P, 2, HV])
        sq = rt[:]
        st6 = at("st6", [P, 2, 6])
        mv = at("mv", [P, 2, 2])
        ve = at("ve", [P, 2])
        rs = at("rs", [P, 2])
        z_at = place[0]
        la = at("la", [P, TPS, HEADS * HK])
        place[0] = z_at
        sz = at("sz", [P, 2, TOK])
        z_at = place[0]
        edec = at("edec", [P, TPS, HEADS * HK])
        ob = at("ob", [P, HV])
        tb = at("tb", [P, 2, HV])
        z_end = place[0]
        place[0] = z_at
        mz = at("mz", [P, 3, TOK])
        assert place[0] <= z_end
        place[0] = z_end
        ga = edec
        aT = at("aT", [HK, HEADS, 2 * TPS])
        ssq = at("ssq", [P, 8])
        vn = at("vn", [P, 8])
        rn = at("rn", [P, 8])
        h2T = mz
        scr = mz[:, :, :].rearrange("p a b -> p (a b)")[:, 0:D]

        place[0] = keep_base
        est = [at(f"est{i}", [P, EPC]) for i in range(EP)]
        assert place[0] <= oT_end
        place[0] = oT_end
        whi = [at(f"whi{i}", [P, EPC], F32R) for i in range(EP)]
        wlo = [at(f"wlo{i}", [P, EPC], F32R) for i in range(EP)]
        gX = at("gX", [TB, D])
        xT = [at(f"xT{i}", [P, DC, TB], F32R) for i in range(2)]
        sgate = at("sgate", [TB, DE])
        hid = at("hid", [TB, DE])
        hidT = [at(f"hidT{i}", [P, EC, TB], F32R) for i in range(2)]
        yS = at("yS", [TB, D])
        tix = at("tix", [TB, 2], I32)
        pix = at("pix", [TB, 2], I32)
        gfin = at("gfin", [P, D])
        wvec = at("wvec", [P, 2, TILES])
        dst = at("dst", [P, 2, TILES], I32)

        meta = at("meta", [1, 72], I32)
        moe_end = place[0]
        place[0] = oT_end

        gm8 = at("gm8", [P, TILES, 8])
        gi8 = at("gi8", [P, TILES, 8], U32)
        gif = at("gif", [P, TILES])
        gmask = at("gmask", [P, TILES, EXPERTS])
        pen = at("pen", [P, TILES, EXPERTS])
        lm = at("lm", [P, TILES, EXPERTS])
        em8 = at("em8", [P, TILES, 8])
        ei8 = at("ei8", [P, TILES, 8], U32)
        eif = at("eif", [P, TILES, 2])
        ngm = at("ngm", [P, TILES, GROUPS])
        gex = at("gex", [P, TILES, GROUPS])
        gsum = at("gsum", [P, TILES])
        pg = at("pg", [P, TILES])
        dd = at("dd", [P, TILES])
        ex = at("ex", [P, TILES])
        den = at("den", [P, TILES])
        g1 = at("g1", [P, TILES])
        g2 = at("g2", [P, TILES])
        oh = [at(f"oh{k}", [P, TILES, EXPERTS]) for k in range(2)]
        both = at("both", [P, TILES, EXPERTS])
        runs = at("runs", [P, TILES + 1, EXPERTS])
        ones = at("ones", [P, P])
        cntc = at("cntc", [EXPERTS, 1])
        cmp = at("cmp", [EXPERTS, MAX_PER_EXPERT])
        nbc = at("nbc", [EXPERTS, 1])
        nbb = at("nbb", [EXPERTS, P])
        bend = at("bend", [EXPERTS, 1])
        bcmp = at("bcmp", [EXPERTS, 64])
        pstart = at("pstart", [P, EXPERTS])
        rank = at("rank", [P, TILES, EXPERTS])
        pick = at("pick", [P, TILES, EXPERTS])
        dstf = at("dstf", [P, 2, TILES])
        tokid = at("tokid", [P, TILES, 2, 2], I32)
        metaf = at("metaf", [1, 72])
        assert place[0] <= oT_end + 4 * 2 * EP * EPC
        place[0] = moe_end
        place[0] = keep_base
        cx = [at(f"cx{i}", [P, D]) for i in range(3)]
        cy = [at(f"cy{i}", [P, 2 * D]) for i in range(3)]
        co = [at(f"co{i}", [P, D]) for i in range(3)]
        cq = at("cq", [P, 3 * TILES])
        cscr = at("cscr", [P, D])
        assert place[0] <= oT_end + 4 * 2 * EP * EPC
        ps = ctx.enter_context(nc.psum_tensor("ps", [P, 8, 512], F32))

        ident = cst[:, C_IDENT:C_IDENT + P]
        GB = [6, 2, 4]

        cst_in = sem("cst_in")
        ones_set = sem("ones_set")
        g_scaled = sem("g_scaled")
        x_in = [sem(f"x_in{j}") for j in range(TPS)]
        xr_in = [sem(f"xr_in{j}") for j in range(TPS)]
        w_in = [sem(f"w_in{i}") for i in range(STAGE)]
        w_hi = sem("w_hi")
        w_lo = sem("w_lo")
        vec_step = sem("vec_step")
        pool_step = sem("pool_step")
        n1_sum = sem("n1_sum")
        n1_rstd = sem("n1_rstd")
        n1_h = sem("n1_h")
        n1_tr = sem("n1_tr")
        hT_hi = sem("hT_hi")
        hT_lo = sem("hT_lo")
        glr_mm = sem("glr_mm")
        glr_cp = sem("glr_cp")
        gate_mm = sem("gate_mm")
        gate_cp = sem("gate_cp")
        gate_l = sem("gate_l")
        gate_la = sem("gate_la")
        dec_mm = sem("dec_mm")
        dec_e = sem("dec_e")
        proj = sem("proj")
        p_cp = sem("p_cp")
        silu = sem("silu")
        rot = sem("rot")
        kd_done = sem("kd_done")
        sgn_pool = sem("sgn_pool")
        tr_u = sem("tr_u")
        qkT_cp = sem("qkT_cp")
        s_upd = sem("s_upd")
        score = sem("score")
        sT_cp = sem("sT_cp")
        o_mm = sem("o_mm")
        pe_seen = sem("pe_seen")
        stat = sem("stat")
        t_vec = sem("t_vec")
        rstd = sem("rstd")
        og_act = sem("og_act")
        o_tr = sem("o_tr")
        oT_hi = sem("oT_hi")
        oT_lo = sem("oT_lo")
        zr_mm = sem("zr_mm")
        br_mm = sem("br_mm")
        z_sig = sem("z_sig")
        m_part = sem("m_part")
        m_sum = sem("m_sum")
        mT_hi = sem("mT_hi")
        mT_lo = sem("mT_lo")
        out_mm = sem("out_mm")
        x2_add = sem("x2_add")
        n2_sum = sem("n2_sum")
        n2_rstd = sem("n2_rstd")
        n2_h = sem("n2_h")
        n2_tr = sem("n2_tr")
        n2_cp = sem("n2_cp")
        log_mm = sem("log_mm")
        log_add = sem("log_add")
        x2_st = [sem(f"x2_st{j}") for j in range(TPS)]
        h2_st = [sem(f"h2_st{j}") for j in range(TPS)]
        raw_st = sem("raw_st")
        fin_st = sem("fin_st")

        cst3 = lambda c, n: cst[:, c:c + n]

        part = ExitStack()
        block = part.enter_context(nc.Block())

        def tot(s, per, n):
            return s * per + (SEED + n)

        V = slice(2 * HK, 2 * HK + HV)
        G = slice(2 * HK + HV, HW)
        B_T, B_U, B_S, B_O, B_OT, B_G = 2, 3, 4, 5, 6, 7

        def qT(k, c0, c1):
            o = (k % 2) * 2 * P if k < RET_ITEMS else (k % 4) * P
            return qkT[:, o + c0:o + c1]

        def used(s, w):
            if w < 0:
                return out_mm, s * (3 * TPS) + (SEED + (w + 1) * TPS)
            if w < W_HEAD:
                return glr_mm, s + (SEED + 1)
            if w < W_Z:
                return proj, s * ITEMS + (SEED + (w - W_HEAD + 1) * TPS)
            if w < W_OUT:
                return br_mm, s * DC + (w - W_Z + 1)
            return out_mm, s * (3 * TPS) + (SEED + (w - W_OUT + 1) * TPS)

        @block.sync
        def _(sp):
            sp.dma_start(cst[:], consts).then_inc(cst_in, 16)
            for j in range(TPS):
                sp.dma_start(H[j][:], x_all[j]).then_inc(x_in[j], 16)
            for dst_, src_ in ((gmix[:], g_mix.partition_broadcast(P)), (gffn[:], g_ffn.partition_broadcast(P)),
                               (ggla[:], g_gla.partition_broadcast(P)), (rb[:], b_router.partition_broadcast(P)),
                               (gk2s[:], gk2), (wr[:], w_router), (S0[:], states)):
                sp.dma_start(dst_, src_).then_inc(cst_in, 16)
            with sp.Fori(0, SUPER) as s:
                for r in range(NP_SB):
                    if r == PIECE0[W_Z]:
                        sp.wait_ge(n2_h, s * TPS + SEED)
                        for j in range(TPS):
                            rows = x_all[bass.ds(s * TPS + j, 1)].rearrange("o p d -> p (o d)")
                            sp.wait_ge(x2_st[j], s * 16 + 16)
                            sp.dma_start(XR[j][:], rows).then_inc(xr_in[j], 16)
                        sp.wait_ge(n1_tr, tot(s, TPS, TPS))
                        sp.wait_ge(n2_tr, s * TPS + SEED)
                        for j in range(TPS):
                            rows = x_all[bass.ds(s * TPS + (TPS + j), 1)].rearrange("o p d -> p (o d)")
                            sp.wait_ge(h2_st[j], s * 16 + 16)
                            sp.dma_start(H[j][:], rows).then_inc(x_in[j], 16)
                    sp.wait_ge(w_lo, s * NP_SB + (SEED + r - STAGE + 1))
                    sp.dma_start(stage[r % STAGE][:], wmix[r]).then_inc(w_in[r % STAGE], 16)
            sp.wait_ge(s_upd, SUPER * ITEMS + SEED)
            sp.dma_start(fin_out, S0[:]).then_inc(fin_st, 16)
            sp.wait_ge(fin_st, 16)
            sp.wait_ge(raw_st, 16 * (2 * SUPER + 1))
            for j in range(TPS):
                sp.wait_ge(x2_st[j], 16 * (SUPER + 1))
                sp.wait_ge(h2_st[j], 16 * (SUPER + 1))

        @block.scalar
        def _(act):
            def rms_sum(j, s_, first):
                act.wait_ge(x_in[j], s_ * 16 + 16)
                if not first:
                    act.wait_ge(n1_sum, s_ * TPS + j)
                    act.wait_ge(n2_sum, (s_ - 1) * TPS + SEED)
                elif j:
                    act.wait_ge(n1_sum, j)
                act.activation(scr, H[j][:], ACT.Square, accum_out=ssq[:, j:j + 1]).then_inc(n1_sum, 1)

            def hT_evac(j, s_):
                for g in range(2):
                    if g == 0:
                        act.wait_ge(n1_tr, tot(s_, TPS, j + 1))
                    act.activation(hT[0][:, 4 * g:4 * g + 4, j * P:(j + 1) * P],
                                   ps[:, GB[j] + g, :].rearrange("p (c t) -> p c t", c=4), ACT.Copy)\
                       .then_inc(hT_hi, 1)

            def split_hi(w, s):
                for q in range(PIECES[w]):
                    r = PIECE0[w] + q
                    act.wait_ge(w_in[r % STAGE], s * (16 * (NP_SB // STAGE)) + 16 * (r // STAGE + 1))
                    if q == 0:
                        act.wait_ge(*used(s, w - 2))
                    act.activation(whl[w % 2][0][:, q * PIECE:(q + 1) * PIECE], stage[r % STAGE][:], ACT.Copy)\
                       .then_inc(w_hi, 1)
                    yield

            act.wait_ge(cst_in, 16 * 8)
            for k_, sm_ in ((SEED, p_cp), (SEED, silu), (SEED, qkT_cp), (SEED, z_sig), (SEED, og_act), (SEED, n2_sum),
                            (SEED, oT_hi), (SEED, mT_hi), (SEED, w_hi), (SEED, hT_hi), (SEED, gate_cp), (SEED, gate_l), (SEED, dec_e)):
                act.sem_inc(sm_, k_)
            for j in range(TPS):
                rms_sum(j, 0, True)
            for j in range(TPS):
                hT_evac(j, 0)
            with act.Fori(0, SUPER) as s:
                for _ in split_hi(0, s):
                    pass
                for _ in split_hi(1, s):
                    pass
                splits = iter(())
                for i in range(ITEMS + 5):
                    if i < ITEMS:
                        if i % TPS == 0 and i // TPS + 2 < W_OUT + 9:
                            splits = split_hi(i // TPS + 2, s)
                        act.wait_ge(proj, tot(s, ITEMS, i + 1))
                        act.wait_ge(o_mm, s * ITEMS + (SEED + i - 3))
                        act.wait_ge(t_vec, s * ITEMS + (SEED + i - 3))
                        act.activation(pS[:, i % 4, :], ps[:, i % 2, 0:HW], ACT.Copy).then_inc(p_cp, 1)
                        act.wait_ge(p_cp, tot(s, ITEMS, i + 1))
                        act.activation(pS[:, i % 4, G], pS[:, i % 4, G], ACT.Silu).then_inc(silu, 1)
                    if 1 <= i <= ITEMS:
                        k = i - 1
                        act.wait_ge(tr_u, tot(s, ITEMS, k + 1))
                        n = 2 * P if k < RET_ITEMS else P
                        free = k - 1 if k < RET_ITEMS else max(k - 3, RET_ITEMS - 1 + (k - RET_ITEMS) // 2)
                        act.wait_ge(o_mm, s * ITEMS + (SEED + free))
                        act.activation(qT(k, 0, n), ps[0:HK, B_T, 0:n], ACT.Copy,
                                       scale=1.0 if k < RET_ITEMS else HK ** -0.5).then_inc(qkT_cp, 1)
                    if 3 <= i <= ITEMS + 2:
                        k = i - 3
                        act.wait_ge(o_mm, tot(s, ITEMS, k + 1))
                        if k >= RET_ITEMS:
                            act.wait_ge(stat, s * ITEMS + k)
                            act.activation(sq, ps[:, B_O, 0:HV], ACT.Square,
                                           accum_out=mv[:, k % 2, 1:2]).then_inc(stat, 1)
                        act.wait_ge(t_vec, tot(s, ITEMS, k + 1))
                        act.wait_ge(rstd, tot(s, ITEMS, k + 1))
                        act.wait_ge(o_tr, s * ITEMS + (SEED + k - 1))
                        act.activation(og[:, k % 2, :], tb[:, k % 2, :], ACT.Copy, scale=rs[:, k % 2:k % 2 + 1])\
                           .then_inc(og_act, 1)
                    if i in (RET_ITEMS - 1, ITEMS - 1):
                        m = 0 if i < RET_ITEMS else 1
                        act.wait_ge(s_upd, tot(s, ITEMS, i - 1))
                        act.dma_start(raw_out[bass.ds(s * 2 + m, 1)].rearrange("o k h v -> k (o h v)"),
                                      RAW[:, :, :].rearrange("k h v -> k (h v)")).then_inc(raw_st, 16)
                    if 4 <= i <= ITEMS + 3:
                        k = i - 4
                        act.wait_ge(o_tr, tot(s, ITEMS, k + 1))
                        act.activation(oT[0][:, k // TPS, (k % TPS) * P:(k % TPS + 1) * P],
                                       ps[:, B_OT, 0:P], ACT.Copy).then_inc(oT_hi, 1)
                    if i == 0:
                        act.wait_ge(glr_mm, s + (SEED + 1))
                        act.activation(glrT[0:RANK, :], ps[0:RANK, B_G, 0:TOK], ACT.Copy).then_inc(glr_cp, 1)
                    if i == 1:
                        act.wait_ge(gate_mm, s * 2 + (SEED + 1))
                        act.activation(la[:, 0:2, :].rearrange("p t n -> p (t n)"), ps[:, B_G, :], ACT.Copy)\
                           .then_inc(gate_cp, 1)
                    if i == 2:
                        act.wait_ge(gate_mm, s * 2 + (SEED + 2))
                        act.activation(la[:, 2, :], ps[:, B_G, 0:256], ACT.Copy).then_inc(gate_cp, 1)
                        act.wait_ge(gate_cp, s * 2 + (SEED + 2))
                        laf, gaf = (x[:, :, :].rearrange("p t n -> p (t n)") for x in (la, ga))
                        act.activation(gaf, laf, ACT.Abs).then_inc(gate_l, 1)
                        act.wait_ge(gate_l, s * 3 + (SEED + 1))
                        act.activation(gaf, gaf, ACT.Exp, scale=-1.0).then_inc(gate_l, 1)
                        act.wait_ge(gate_l, s * 3 + (SEED + 2))
                        act.activation(gaf, gaf, ACT.Ln, bias=1.0).then_inc(gate_l, 1)
                    if i == 5:
                        act.wait_ge(dec_mm, s * 2 + (SEED + 1))
                        act.activation(edec[:, 0:2, :].rearrange("p t n -> p (t n)"), ps[:, B_G, :], ACT.Exp)\
                           .then_inc(dec_e, 1)
                    if i == 6:
                        act.wait_ge(dec_mm, s * 2 + (SEED + 2))
                        act.activation(edec[:, 2, :], ps[:, B_G, 0:256], ACT.Exp).then_inc(dec_e, 1)
                        act.activation(aT[:, :, :].rearrange("p h c -> p (h c)"),
                                       ps[0:HK, B_G, 256:256 + HEADS * 2 * TPS], ACT.Exp).then_inc(dec_e, 1)
                    for _ in splits:
                        break
                def mt_evac(d):
                    act.wait_ge(m_sum, tot(s, DC, d + 1))
                    act.activation(mT[0][:, d, :], mz[:, 2, :], ACT.Copy).then_inc(mT_hi, 1)
                for d in range(DC):
                    w = W_Z + d
                    b0 = [(0, 1, 6, 7), (2, 3, 4, 5)][d % 2]
                    act.wait_ge(m_part, s * DC + (SEED + d))
                    act.wait_ge(zr_mm, s * 2 * DC + (SEED + 2 * d + 1))
                    act.activation(sz[:, 0, :], ps[:, b0[0], 0:TOK], ACT.Sigmoid)
                    act.wait_ge(zr_mm, s * 2 * DC + (SEED + 2 * d + 2))
                    act.activation(sz[:, 1, :], ps[:, b0[1], 0:TOK], ACT.Sigmoid).then_inc(z_sig, 1)
                    for _ in split_hi(w + 1, s):
                        pass
                    mt_evac(d)
                for _ in split_hi(W_OUT + 1, s):
                    pass
                act.wait_ge(mT_lo, tot(s, DC, DC))
                for j in range(TPS):
                    rms_sum(j, s + 1, False)
                for _ in split_hi(W_OUT + 2, s):
                    pass
                for j in range(TPS):
                    act.wait_ge(x2_add, s * 3 * TPS + (SEED + 2 * TPS + j + 1))
                    act.wait_ge(n1_sum, s * TPS + 2 * TPS)
                    act.wait_ge(n2_sum, tot(s, TPS, j))
                    act.activation(scr, XR[j][:], ACT.Square, accum_out=ssq[:, 3 + j:4 + j]).then_inc(n2_sum, 1)
                for j in range(TPS):
                    hT_evac(j, s + 1)
                for j in range(TPS):
                    act.dma_start(x2_dram[bass.ds(s * TPS + j, 1)].rearrange("o p d -> p (o d)"), XR[j][:])\
                       .then_inc(x2_st[j], 16)
                    act.wait_ge(n2_h, tot(s, TPS, j + 1))
                    act.dma_start(h2_dram[bass.ds((s * TPS + j) * P, P)], H[j][:]).then_inc(h2_st[j], 16)
                for j in range(TPS):
                    act.wait_ge(n2_tr, tot(s, TPS, j + 1))
                    act.wait_ge(log_mm, s * TPS + (SEED + j))
                    act.activation(h2T[:, :, :].rearrange("p a b -> p (a b)")[:, 0:D],
                                   ps[:, GB[j]:GB[j] + 2, :].rearrange("p b n -> p (b n)"), ACT.Copy).then_inc(n2_cp, 1)

        @block.gpsimd
        def _(pool):
            def rms(j, col, total, out_sem, in_sem, value):
                pool.wait_ge(in_sem, value)
                pool.tensor_tensor(vn[:, col:col + 1], ssq[:, col:col + 1], half[:, 3:4], ALU.add)\
                    .then_inc(pool_step, 1)
                step[0] += 1
                pool.wait_ge(pool_step, step[0])
                pool.tensor_tensor(rn[:, col:col + 1], vn[:, col:col + 1], half[:, 0:1], ALU.pow).then_inc(out_sem, 1)

            step = [0]
            pool.memset(half[:, 0:1], -0.5).then_inc(pool_step, 1)
            for f, value in enumerate((EPS, EPS * HV, EPS * D)):
                pool.memset(half[:, f + 1:f + 2], value).then_inc(pool_step, 1)
            pool.memset(kd[:], 0.0).then_inc(pool_step, 1)
            pool.wait_ge(pool_step, 5)
            step[0] = 5
            pool.wait_ge(g_scaled, 3)
            for sm_ in (kd_done, sgn_pool, rstd, m_sum, n2_rstd):
                pool.sem_inc(sm_, SEED)
            for j in range(TPS):
                rms(j, j, None, n1_rstd, n1_sum, j + 1)
            with pool.Fori(0, SUPER) as s:
                pool.sem_clear(pool_step)
                step[0] = 0
                for i in range(ITEMS + 4):

                    if i < ITEMS:
                        h = i // TPS
                        if i < RET_ITEMS:
                            pool.wait_ge(tr_u, s * ITEMS + (SEED + i - 1))
                            pool.wait_ge(rot, s * RET_ITEMS + (SEED + i + 1))
                            for c in range(2):
                                f = C_KDEC + c * HEADS + h
                                ins = pool.tensor_tensor(kd[:, i % 2, c, :], qk[:, i % 2, HK:2 * HK],
                                                         cst[:, f:f + 1].to_broadcast([P, HK]), ALU.mult)
                            ins.then_inc(kd_done, 1)
                        else:
                            pool.wait_ge(silu, tot(s, ITEMS, i + 1))
                            pool.tensor_tensor(pS[:, i % 4, G], pS[:, i % 4, G], ggla[:], ALU.mult).then_inc(sgn_pool, 1)
                    if 3 <= i <= ITEMS + 2:
                        k = i - 3
                        pool.wait_ge(stat, s * ITEMS + (k + 1))
                        pool.wait_ge(og_act, s * ITEMS + (SEED + k - 1))
                        f = 1 if k < RET_ITEMS else 2
                        pool.tensor_tensor(ve[:, k % 2:k % 2 + 1], mv[:, k % 2, 1:2], half[:, f:f + 1], ALU.add)\
                            .then_inc(pool_step, 1)
                        step[0] += 1
                        pool.wait_ge(pool_step, step[0])
                        pool.tensor_tensor(rs[:, k % 2:k % 2 + 1], ve[:, k % 2:k % 2 + 1], half[:, 0:1], ALU.pow)\
                            .then_inc(rstd, 1)
                for d in range(DC):
                    pool.wait_ge(m_part, tot(s, DC, d + 1))
                    pool.wait_ge(mT_lo, s * DC + (SEED + d))
                    pool.tensor_tensor(mz[:, 2, :], mz[:, 0, :], mz[:, 1, :], ALU.add).then_inc(m_sum, 1)
                for j in range(TPS):
                    rms(j, j, None, n1_rstd, n1_sum, s * TPS + (TPS + j + 1))
                for j in range(TPS):
                    rms(j, 3 + j, None, n2_rstd, n2_sum, tot(s, TPS, j + 1))


        @block.vector
        def _(vec):
            step = [0]

            def mark(ins):
                step[0] += 1
                ins.then_inc(vec_step, 1)
                return step[0]

            def norm1(j, s_):
                vec.wait_ge(n1_rstd, s_ * TPS + (j + 1))
                vec.scalar_tensor_tensor(H[j][:], H[j][:], rn[:, j:j + 1], gmix[:], ALU.mult, ALU.mult)\
                   .then_inc(n1_h, 1)

            def hT_lo_part(j, s_):
                for g in range(2):
                    vec.wait_ge(hT_hi, s_ * (2 * TPS) + (SEED + 2 * j + g + 1))
                    o = (slice(None), slice(4 * g, 4 * g + 4), slice(j * P, (j + 1) * P))
                    vec.tensor_tensor(hT[1][o], ps[:, GB[j] + g, :].rearrange("p (c t) -> p c t", c=4),
                                      hT[0][o].bitcast(F32), ALU.subtract).then_inc(hT_lo, 1)

            def split_lo(w, s):
                for q in range(PIECES[w]):
                    r = PIECE0[w] + q
                    vec.wait_ge(w_hi, s * NP_SB + (SEED + r + 1))
                    o = (slice(None), slice(q * PIECE, (q + 1) * PIECE))
                    vec.tensor_tensor(whl[w % 2][1][o], stage[r % STAGE][:], whl[w % 2][0][o].bitcast(F32),
                                      ALU.subtract).then_inc(w_lo, 1)
                    yield

            vec.wait_ge(cst_in, 16 * 8)
            for sm_ in (w_lo, rot, sT_cp, s_upd, t_vec, oT_lo, m_part, mT_lo, x2_add, n2_h, log_add, hT_lo):
                vec.sem_inc(sm_, SEED)
            for w_, n_ in ((gmix, D), (gffn, D), (ggla, HV)):
                vec.tensor_scalar(w_[:], w_[:], float(n_) ** 0.5, None, ALU.mult).then_inc(g_scaled, 1)
            vec.wait_ge(g_scaled, 3)
            vec.memset(keep[:], 0.0).then_inc(vec_step, 1)
            vec.memset(glrT[:], 1.0).then_inc(ones_set, 1)
            vec.memset(logits[:, :, 36:40], -BIG).then_inc(vec_step, 1)
            vec.wait_ge(vec_step, 2)
            for j in range(TPS):
                norm1(j, 0)
            for j in range(TPS):
                hT_lo_part(j, 0)
            with vec.Fori(0, SUPER) as s:
                vec.sem_clear(vec_step)
                step[0] = 0
                for _ in split_lo(0, s):
                    pass
                for _ in split_lo(1, s):
                    pass
                splits = iter(())
                for i in range(ITEMS + 5):
                    if i < ITEMS:
                        h, j = i // TPS, i % TPS
                        if j == 0:
                            splits = split_lo(h + 2, s)
                        if i < RET_ITEMS:
                            vec.wait_ge(p_cp, tot(s, ITEMS, i + 1))
                            vec.wait_ge(tr_u, s * ITEMS + (SEED + i - 1))
                            x4 = pS[:, i % 4, 0:2 * HK].rearrange("p (a b c) -> p a b c", a=2, b=2)
                            rtab = cst[:, bass.ds(s * (TPS * ROT) + (C_ROT + j * ROT), ROT)]
                            cos = rtab[:, 0:32]
                            qk4 = qk[:, i % 2, :].rearrange("p (a b c) -> p a b c", a=2, b=2)
                            rt4 = rt[:].rearrange("p (a b c) -> p a b c", a=2, b=2)
                            mark(vec.tensor_tensor(qk4, x4, cos.unsqueeze(1).unsqueeze(1).to_broadcast([P, 2, 2, 32]), ALU.mult))
                            vec.wait_ge(rot, s * RET_ITEMS + (SEED + i))
                            for b in range(2):
                                sn = rtab[:, 32 + 32 * b:64 + 32 * b]
                                a_ = mark(vec.tensor_tensor(rt4[:, :, b, :], x4[:, :, 1 - b, :],
                                                            sn.unsqueeze(1).to_broadcast([P, 2, 32]), ALU.mult))
                            vec.wait_ge(vec_step, a_)
                            vec.tensor_tensor(qk[:, i % 2, :], qk[:, i % 2, :], rt[:], ALU.add).then_inc(rot, 1)
                        else:
                            vec.wait_ge(p_cp, tot(s, ITEMS, i + 1))
                            vec.wait_ge(tr_u, s * ITEMS + (SEED + i - 1))
                            vec.wait_ge(dec_e, s * 3 + (SEED + 3))
                            hh = (h - HEADS) * HK
                            for c in range(2):
                                r = slice(c * CHUNK, (c + 1) * CHUNK)
                                ins = vec.tensor_tensor(kd[r, i % 2, c, :], pS[r, i % 4, HK:2 * HK],
                                                        edec[r, j, hh:hh + HK], ALU.mult)
                            ins.then_inc(kd_done, 1)
                    if 1 <= i <= ITEMS:
                        k = i - 1
                        h, j = k // TPS, k % TPS
                        vec.wait_ge(tr_u, tot(s, ITEMS, k + 1))
                        vec.wait_ge(o_mm, s * ITEMS + (SEED + k - (1 if j == TPS - 1 else 2)))
                        if h >= HEADS:
                            vec.wait_ge(dec_e, s * 3 + (SEED + 3))
                        cur = S0[:, h, :] if j == 0 else SW[:, (k - 1) % 4, 1, :]
                        for c in range(2):
                            u = ps[0:HK, B_U, c * HV:(c + 1) * HV]
                            if j == 0 and c == 0:
                                if h % HEADS == 0:
                                    vec.wait_ge(raw_st, s * 32 + (16 + h // HEADS * 16))
                                nxt = RAW[:, h % HEADS, :]
                            elif c == 0:
                                nxt = SW[:, k % 4, 0, :]
                            elif j == TPS - 1:
                                nxt = S0[:, h, :]
                            else:
                                nxt = SW[:, k % 4, 1, :]
                            if h < HEADS:
                                dec = float(np.exp(CHUNK * np.log1p(-np.exp2(-5.0 - h))))
                            else:
                                dec = aT[:, h - HEADS, 2 * j + c:2 * j + c + 1]
                            if c == 0 and j > 0:
                                vec.wait_ge(s_upd, s * ITEMS + (SEED + k))
                            ins = vec.scalar_tensor_tensor(nxt, cur, dec, u, ALU.mult, ALU.add)
                            if c == 1:
                                ins.then_inc(s_upd, 1)
                                break
                            vec.wait_ge(vec_step, mark(ins))
                            cur = nxt
                            if j == 0:
                                nxt = SW[:, k % 4, 0, :]
                                vec.wait_ge(vec_step, mark(vec.tensor_scalar(nxt, cur, keep[:], None, ALU.mult)))
                                cur = nxt
                    if 2 <= i <= RET_ITEMS + 1:
                        k = i - 2
                        vec.wait_ge(score, s * RET_ITEMS + (SEED + k + 1))
                        vec.wait_ge(o_mm, s * ITEMS + (SEED + k))
                        hh = k // TPS
                        vec.tensor_tensor(sT[:], ps[:, B_S, 0:P], cst3(C_DMAT + hh * P, P), ALU.mult)\
                           .then_inc(sT_cp, 1)
                    if 3 <= i <= ITEMS + 2:
                        k = i - 3
                        vec.wait_ge(o_mm, tot(s, ITEMS, k + 1))
                        vec.wait_ge(og_act, s * ITEMS + (SEED + k - 1))
                        if k < RET_ITEMS:
                            hh = k // TPS
                            vec.wait_ge(vec_step, mark(vec.tensor_scalar(
                                ob[:], ps[:, B_O, 0:HV], cst[:, C_QDEC + hh:C_QDEC + hh + 1], None, ALU.mult)))
                            vec.wait_ge(vec_step, mark(vec.tensor_tensor(ob[:], ob[:], ps[:, B_O, HV:2 * HV], ALU.add)))
                            a_ = mark(vec.bn_stats(st6[:, k % 2, :], ob[:]))
                            vec.wait_ge(vec_step, a_)
                            vec.wait_ge(rstd, s * ITEMS + (SEED + k - 1))
                            vec.bn_aggr(mv[:, k % 2, :], st6[:, k % 2, :]).then_inc(stat, 1)
                            vec.wait_ge(stat, s * ITEMS + (k + 1))
                            vec.wait_ge(silu, tot(s, ITEMS, k + 1))
                            vec.scalar_tensor_tensor(tb[:, k % 2, :], ob[:], mv[:, k % 2, 0:1], pS[:, k % 4, G],
                                                     ALU.subtract, ALU.mult).then_inc(t_vec, 1)
                        else:
                            vec.wait_ge(sgn_pool, s * (ITEMS - RET_ITEMS) + (SEED + k - RET_ITEMS + 1))
                            vec.wait_ge(stat, s * ITEMS + (k + 1))
                            vec.tensor_tensor(tb[:, k % 2, :], ps[:, B_O, 0:HV], pS[:, k % 4, G], ALU.mult)\
                               .then_inc(t_vec, 1)
                    if 4 <= i <= ITEMS + 3:
                        k = i - 4
                        vec.wait_ge(oT_hi, tot(s, ITEMS, k + 1))
                        o = (slice(None), k // TPS, slice((k % TPS) * P, (k % TPS + 1) * P))
                        vec.tensor_tensor(oT[1][o], ps[:, B_OT, 0:P], oT[0][o].bitcast(F32), ALU.subtract)\
                           .then_inc(oT_lo, 1)
                    if i == 3:
                        laf, gaf = (x[:, :, :].rearrange("p t n -> p (t n)") for x in (la, ga))
                        vec.wait_ge(gate_l, s * 3 + (SEED + 3))
                        vec.wait_ge(vec_step, mark(vec.tensor_scalar(laf, laf, 0.0, None, ALU.min)))
                        vec.wait_ge(vec_step, mark(vec.tensor_tensor(laf, laf, gaf, ALU.subtract)))
                        vec.tensor_scalar(laf, laf, 1.0 / 16.0, None, ALU.mult).then_inc(gate_la, 1)
                    for _ in splits:
                        break
                vec.memset(keep[:], 1.0).then_inc(vec_step, 1)
                step[0] += 1
                for d in range(DC):
                    b0 = [(0, 1, 6, 7), (2, 3, 4, 5)][d % 2]
                    for _ in split_lo(W_Z + d + 1, s):
                        pass
                    vec.wait_ge(z_sig, tot(s, DC, d + 1))
                    vec.wait_ge(br_mm, s * DC + (d + 1))
                    vec.wait_ge(m_sum, s * DC + (SEED + d))
                    mark(vec.tensor_tensor(mz[:, 0, :], sz[:, 0, :], ps[:, b0[2], 0:TOK], ALU.mult))
                    vec.tensor_tensor(mz[:, 1, :], sz[:, 1, :], ps[:, b0[3], 0:TOK], ALU.mult).then_inc(m_part, 1)
                    vec.wait_ge(mT_hi, tot(s, DC, d + 1))
                    vec.tensor_tensor(mT[1][:, d, :], mz[:, 2, :], mT[0][:, d, :].bitcast(F32), ALU.subtract)\
                       .then_inc(mT_lo, 1)
                for n, (c0, cn) in enumerate(OUT_COLS):
                    if n < 2:
                        for _ in split_lo(W_OUT + n + 1, s):
                            pass
                    for j in range(TPS):
                        vec.wait_ge(out_mm, s * 3 * TPS + (SEED + n * TPS + j + 1))
                        vec.wait_ge(xr_in[j], s * 16 + 16)
                        vec.tensor_tensor(XR[j][:, c0:c0 + cn], XR[j][:, c0:c0 + cn],
                                          ps[:, (n * TPS + j) % 2, 0:cn], ALU.add).then_inc(x2_add, 1)
                    if n == 1:
                        for j in range(TPS):
                            norm1(j, s + 1)
                for j in range(TPS):
                    hT_lo_part(j, s + 1)
                    vec.wait_ge(n2_rstd, tot(s, TPS, j + 1))
                    vec.wait_ge(n1_tr, s * TPS + (SEED + TPS + j + 1))
                    vec.wait_ge(x2_add, s * 3 * TPS + (SEED + 2 * TPS + j + 1))
                    vec.scalar_tensor_tensor(H[j][:], XR[j][:], rn[:, 3 + j:4 + j], gffn[:], ALU.mult, ALU.mult)\
                       .then_inc(n2_h, 1)
                for j in range(TPS):
                    vec.wait_ge(log_mm, tot(s, TPS, j + 1))
                    vec.tensor_tensor(logits[:, bass.ds(s * TPS + j, 1), 0:36].rearrange("p o n -> p (o n)"),
                                      ps[:, j % 2, 0:36], rb[:], ALU.add).then_inc(log_add, 1)

        def z_banks(d):
            return [(0, 1, 6, 7), (2, 3, 4, 5)][d % 2]

        def z_part(pe, s, d, x, three):
            w = W_Z + d
            if x == 0:
                pe.wait_ge(w_lo, s * NP_SB + (SEED + PIECE0[w] + PIECES[w]))
                if d == 0:
                    pe.wait_ge(p_cp, tot(s, ITEMS, ITEMS))
                elif d == 1:
                    pe.wait_ge(oT_lo, tot(s, ITEMS, ITEMS))
                else:
                    pe.wait_ge(m_part, s * DC + (SEED + d - 1))
            W = [whl[w % 2][i][:, x * PIECE:(x + 1) * PIECE].rearrange("p (c n) -> p c n", c=DC) for i in range(2)]
            A3 = slice(None)
            for c in range(DC):
                ins = three(ps[:, z_banks(d)[x], 0:TOK], W, hT, (A3, c, A3), (A3, c, A3), c == 0, c == DC - 1)
            ins.then_inc(zr_mm, 1)

        def br_part(pe, s, d, three):
            w = W_Z + d
            if d == 0:
                pe.wait_ge(oT_lo, tot(s, ITEMS, ITEMS))
                pe.wait_ge(dec_e, s * 3 + (SEED + 3))
            A3 = slice(None)
            W = [whl[w % 2][i][:, 2 * PIECE:3 * PIECE].rearrange("p (c n) -> p c n", c=DC) for i in range(2)]
            for x in range(2):
                for c in range(HEADS):
                    ins = three(ps[:, z_banks(d)[2 + x], 0:TOK], W, oT, (A3, x * HEADS + c, A3), (A3, x * HEADS + c, A3),
                                c == 0, c == HEADS - 1)
            ins.then_inc(br_mm, 1)

        @block.tensor
        def _(pe):
            def three(out, A, B, ka, kb, start, stop):
                pe.matmul(out, A[0][ka], B[0][kb], start=start, stop=False)
                pe.matmul(out, A[0][ka], B[1][kb], start=False, stop=False)
                return pe.matmul(out, A[1][ka], B[0][kb], start=False, stop=stop)

            def transposes(j, src_):
                for c in range(DC):
                    ins = pe.transpose(ps[:, GB[j] + c // 4, (c % 4) * P:(c % 4 + 1) * P],
                                       src_[:, c * P:(c + 1) * P], ident)
                return ins

            A3 = slice(None)
            pe.wait_ge(cst_in, 16 * 8)
            for sm_ in (tr_u, o_mm, o_tr, n1_tr, n2_tr, log_mm, proj, zr_mm, glr_mm, gate_mm, dec_mm, out_mm, score):
                pe.sem_inc(sm_, SEED)
            for sm_ in (*x2_st, *h2_st, raw_st):
                pe.sem_inc(sm_, 16)
            for j in range(TPS):
                pe.wait_ge(n1_h, j + 1)
                transposes(j, H[j]).then_inc(n1_tr, 1)
            with pe.Fori(0, SUPER) as s:
                pe.wait_ge(hT_lo, s * (2 * TPS) + (SEED + 2 * TPS))
                pe.wait_ge(w_lo, s * NP_SB + (SEED + 1))
                pe.wait_ge(log_add, s * TPS + SEED)
                W = [whl[0][i][:, 0:PIECE].rearrange("p (c n) -> p c n", c=DC) for i in range(2)]
                for c in range(DC):
                    ins = three(ps[:, B_G, 0:TOK], W, hT, (A3, c, A3), (A3, c, A3),
                                c == 0, c == DC - 1)
                ins.then_inc(glr_mm, 1)
                for i in range(ITEMS + 4):
                    if i < ITEMS:
                        h, j = i // TPS, i % TPS
                        w = W_HEAD + h
                        if j == 0:
                            pe.wait_ge(w_lo, s * NP_SB + (SEED + PIECE0[w] + PIECES[w]))
                        pe.wait_ge(p_cp, s * ITEMS + (SEED + i - 1))
                        W = [whl[w % 2][x][:].rearrange("p (c n) -> p c n", c=DC) for x in range(2)]
                        for c in range(DC):
                            ins = three(ps[:, i % 2, 0:HW], hT, W, (A3, c, slice(j * P, (j + 1) * P)), (A3, c, A3),
                                        c == 0, c == DC - 1)
                        ins.then_inc(proj, 1)
                    elif i < ITEMS + 2:
                        z_part(pe, s, 0, i - ITEMS, three)
                    if 1 <= i <= ITEMS:
                        k = i - 1
                        pe.wait_ge(p_cp, tot(s, ITEMS, k + 1))
                        pe.wait_ge(kd_done, tot(s, ITEMS, k + 1))
                        pe.wait_ge(qkT_cp, s * ITEMS + (SEED + k))
                        pe.wait_ge(s_upd, s * ITEMS + (SEED + k))
                        for c in range(2):
                            pe.matmul(ps[0:HK, B_U, c * HV:(c + 1) * HV], kd[:, k % 2, c, :], pS[:, k % 4, V],
                                      start=True, stop=True)
                        for x in range(2 if k < RET_ITEMS else 1):
                            ins = pe.transpose(ps[0:HK, B_T, x * P:(x + 1) * P],
                                               qk[:, k % 2, x * HK:(x + 1) * HK] if k < RET_ITEMS else pS[:, k % 4, 0:HK],
                                               ident)
                        ins.then_inc(tr_u, 1)
                    if 2 <= i <= RET_ITEMS + 1:
                        k = i - 2
                        pe.wait_ge(qkT_cp, tot(s, ITEMS, k + 1))
                        pe.wait_ge(sT_cp, s * RET_ITEMS + (SEED + k))
                        pe.matmul(ps[:, B_S, 0:P], qT(k, P, 2 * P), qT(k, 0, P), start=True, stop=True).then_inc(score, 1)
                    if 3 <= i <= ITEMS + 2:
                        k = i - 3
                        h, j = k // TPS, k % TPS
                        pe.wait_ge(t_vec, s * ITEMS + (SEED + k))
                        pe.wait_ge(qkT_cp, tot(s, ITEMS, k + 1))
                        pe.wait_ge(s_upd, tot(s, ITEMS, k + 1))
                        if k < RET_ITEMS:
                            pe.wait_ge(sT_cp, tot(s, RET_ITEMS, k + 1))
                            pe.matmul(ps[:, B_O, HV:2 * HV], sT[:], pS[:, k % 4, V], start=True, stop=True)
                        else:
                            pe.sem_inc(pe_seen, 1)
                        for c in range(2):
                            if k < RET_ITEMS:
                                st = SW[:, k % 4, 0, :] if c else (S0[:, h, :] if j == 0 else SW[:, (k - 1) % 4, 1, :])
                            elif c == 0:
                                st = RAW[:, h % HEADS, :] if j == 0 else SW[:, k % 4, 0, :]
                            else:
                                st = S0[:, h, :] if j == TPS - 1 else SW[:, k % 4, 1, :]
                            ins = pe.matmul(ps[c * CHUNK:(c + 1) * CHUNK, B_O, 0:HV],
                                            qT(k, c * CHUNK, (c + 1) * CHUNK), st, start=True, stop=True)
                        ins.then_inc(o_mm, 1)
                    if 4 <= i <= ITEMS + 3:
                        k = i - 4
                        pe.wait_ge(og_act, tot(s, ITEMS, k + 1))
                        pe.wait_ge(oT_lo, s * ITEMS + (SEED + k))
                        pe.transpose(ps[:, B_OT, 0:P], og[:, k % 2, :], ident).then_inc(o_tr, 1)
                    if i in (1, 2):
                        if i == 1:
                            pe.wait_ge(glr_cp, s + 1)
                            pe.wait_ge(ones_set, 1)
                        else:
                            pe.wait_ge(gate_cp, s * 2 + (SEED + 1))
                        for j in ((0, 1), (2,))[i - 1]:
                            ins = pe.matmul(ps[:, B_G, (j % 2) * 256:(j % 2 + 1) * 256],
                                            glrT[0:RANK + 1, j * P:(j + 1) * P], gk2s[:], start=True, stop=True)
                        ins.then_inc(gate_mm, 1)
                    if i in (5, 6):
                        if i == 5:
                            pe.wait_ge(gate_la, s + 1)
                        else:
                            pe.wait_ge(dec_e, s * 3 + (SEED + 1))
                        for j in ((0, 1), (2,))[i - 5]:
                            ins = pe.matmul(ps[:, B_G, (j % 2) * 256:(j % 2 + 1) * 256], cst3(C_TRI, P), la[:, j, :],
                                            start=True, stop=True)
                        if i == 6:
                            for hh in range(HEADS):
                                for j in range(TPS):
                                    o = 256 + hh * 2 * TPS + 2 * j
                                    ins = pe.matmul(ps[0:HK, B_G, o:o + 2], la[:, j, hh * HK:(hh + 1) * HK], cst3(C_IND, 2),
                                                    start=True, stop=True)
                        ins.then_inc(dec_mm, 1)
                for d in range(DC):
                    for x in range(0 if d else 2, 2):
                        z_part(pe, s, d, x, three)
                    br_part(pe, s, d, three)
                for n, (c0, cn) in enumerate(OUT_COLS):
                    w = W_OUT + n
                    pe.wait_ge(w_lo, s * NP_SB + (SEED + PIECE0[w] + PIECES[w]))
                    W = [whl[w % 2][x][:, 0:DC * cn].rearrange("p (c n) -> p c n", c=DC) for x in range(2)]
                    if n == 0:
                        pe.wait_ge(mT_lo, tot(s, DC, DC))
                    for j in range(TPS):
                        o = n * TPS + j
                        if o >= 2:
                            pe.wait_ge(x2_add, s * 3 * TPS + (SEED + o - 1))
                        for c in range(DC):
                            ins = three(ps[:, o % 2, 0:cn], mT, W, (A3, c, slice(j * P, (j + 1) * P)), (A3, c, A3),
                                        c == 0, c == DC - 1)
                        ins.then_inc(out_mm, 1)
                for j in range(TPS):
                    pe.wait_ge(n1_h, s * TPS + (TPS + j + 1))
                    transposes(j, H[j]).then_inc(n1_tr, 1)
                for j in range(TPS):
                    pe.wait_ge(n2_h, tot(s, TPS, j + 1))
                    pe.wait_ge(hT_lo, s * (2 * TPS) + (SEED + 2 * TPS + 2 * j + 2))
                    transposes(j, H[j]).then_inc(n2_tr, 1)
                h2Tf = h2T[:, :, :].rearrange("p a b -> p (a b)")
                pe.wait_ge(x2_add, s * 3 * TPS + (SEED + 3 * TPS))
                for j in range(TPS):
                    pe.wait_ge(n2_cp, s * TPS + (j + 1))
                    if j == 2:
                        pe.wait_ge(log_add, s * TPS + (SEED + 1))
                    for c in range(DC):
                        ins = pe.matmul(ps[:, j % 2, 0:36], h2Tf[:, c * P:(c + 1) * P], wr[:, c, :],
                                        start=(c == 0), stop=(c == DC - 1))
                    ins.then_inc(log_mm, 1)

        r_in = sem("r_in")
        r_vec = sem("r_vec")
        r_exp = sem("r_exp")
        r_ready = sem("r_ready")
        r_mm = sem("r_mm")
        l_init = sem("l_init")
        l_st = sem("l_st")
        part.close()
        block2 = part.enter_context(nc.Block())

        @block2.sync
        def _(sp):
            sp.dma_start(gfin[:], g_final.partition_broadcast(P)).then_inc(r_in, 16)
            sp.dma_start(list_dram, list_init).then_inc(l_init, 16)
            sp.wait_ge(r_in, 16)

        @block2.scalar
        def _(act):
            act.wait_ge(r_ready, 2)
            act.activation(gex[:], ngm[:], ACT.Exp).then_inc(r_exp, 1)
            act.activation(ex[:], dd[:], ACT.Exp).then_inc(r_exp, 1)

        @block2.gpsimd
        def _(pool):
            pool.wait_ge(l_init, 16)
            pool.wait_ge(r_ready, 7)
            for t in range(TILES):
                for k in range(2):
                    pool.indirect_dma_start(out=list_dram, out_offset=bass.IndirectOffsetOnAxis(ap=dst[:, k, t:t + 1], axis=0),
                                            in_=tokid[:, t, k, :], in_offset=None).then_inc(l_st, 16)
            pool.wait_ge(l_st, 16 * 2 * TILES)

        @block2.vector
        def _(vec):
            n = [0]

            def link(ins):
                n[0] += 1
                ins.then_inc(r_vec, 1)
                vec.wait_ge(r_vec, n[0])

            def mark(ins):
                n[0] += 1
                ins.then_inc(r_vec, 1)

            def by_tile(ap):
                return ap.unsqueeze(1).to_broadcast([P, TILES, EXPERTS])

            def by_expert(ap, e=EXPERTS):
                return ap.unsqueeze(2).to_broadcast([P, TILES, e])

            vec.memset(ones[:], 1.0).then_inc(r_ready, 1)
            mark(vec.memset(runs[:, 0, :], 0.0))
            mark(vec.tensor_copy(tokid[:].rearrange("p t k c -> p (t k c)"), cst3(C_TOKID, 4 * TILES)))
            for t in range(TILES):
                mark(vec.max(gm8[:, t, :], logits[:, t, 32:40]))
            vec.wait_ge(r_vec, n[0])
            for t in range(TILES):
                mark(vec.max_index(gi8[:, t, :], gm8[:, t, :], logits[:, t, 32:40]))
            vec.wait_ge(r_vec, n[0])
            link(vec.tensor_copy(gif[:], gi8[:, :, 0]))
            link(vec.tensor_tensor(gmask[:], by_tile(cst3(C_GRP, EXPERTS)), by_expert(gif[:]), ALU.is_equal))
            mark(vec.tensor_scalar(pen[:], gmask[:], BIG, -BIG, ALU.mult, ALU.add))
            link(vec.tensor_tensor(lm[:], logits[:, :, 0:EXPERTS], gmask[:], ALU.mult))
            link(vec.tensor_tensor(lm[:], lm[:], pen[:], ALU.add))
            for t in range(TILES):
                mark(vec.max(em8[:, t, :], lm[:, t, :]))
            vec.wait_ge(r_vec, n[0])
            for t in range(TILES):
                mark(vec.max_index(ei8[:, t, :], em8[:, t, :], lm[:, t, :]))
            vec.wait_ge(r_vec, n[0])
            mark(vec.tensor_tensor(ngm[:], logits[:, :, 32:36], by_expert(gm8[:, :, 0], GROUPS), ALU.subtract))
            vec.tensor_tensor(dd[:], em8[:, :, 1], em8[:, :, 0], ALU.subtract).then_inc(r_ready, 1)
            link(vec.tensor_copy(eif[:], ei8[:, :, 0:2]))
            for k in range(2):
                link(vec.tensor_tensor(oh[k][:], by_tile(cst3(C_IOTA, EXPERTS)), by_expert(eif[:, :, k]), ALU.is_equal))
                link(vec.tensor_tensor(oh[k][:], oh[k][:], by_expert(cst3(C_VALID, TILES)), ALU.mult))
            link(vec.tensor_tensor(both[:], oh[0][:], oh[1][:], ALU.add))
            for t in range(TILES):
                ins = vec.tensor_tensor(runs[:, t + 1, :], runs[:, t, :], both[:, t, :], ALU.add)
                if t < TILES - 1:
                    link(ins)
            ins.then_inc(r_ready, 1)
            vec.wait_ge(r_mm, 1)
            link(vec.tensor_copy(cntc[:], ps[0:EXPERTS, 1, 0:1]))
            link(vec.tensor_scalar(cmp[:], cst[0:EXPERTS, C_STEP:C_STEP + MAX_PER_EXPERT], cntc[:], None, ALU.is_lt))
            link(vec.tensor_reduce(nbc[:], cmp[:], AX.X, ALU.add))
            vec.tensor_scalar(nbb[:], ones[0:EXPERTS, :], nbc[:], None, ALU.mult).then_inc(r_ready, 1)
            vec.wait_ge(r_mm, 2)
            mark(vec.tensor_copy(pstart[:], ps[:, 2, 0:EXPERTS]))
            link(vec.tensor_copy(bend[:], ps[0:EXPERTS, 3, 0:1]))
            vec.tensor_scalar(bcmp[:], cst[0:EXPERTS, C_IOTAB:C_IOTAB + 64], bend[:], None, ALU.is_ge)\
               .then_inc(r_ready, 1)
            link(vec.tensor_tensor(rank[:], ps[:, 0, 0:TILES * EXPERTS].rearrange("p (t e) -> p t e", t=TILES),
                                   by_tile(pstart[:]), ALU.add))
            for k in range(2):
                link(vec.tensor_tensor(pick[:], oh[k][:], rank[:], ALU.mult))
                link(vec.tensor_reduce(dstf[:, k, :], pick[:], AX.X, ALU.add))

            link(vec.tensor_tensor(dstf[:], dstf[:], cst3(C_DUMP, 2 * TILES).rearrange("p (k t) -> p k t", k=2), ALU.add))
            vec.wait_ge(r_mm, 3)
            link(vec.tensor_scalar(metaf[:, 0:64], ps[0:1, 4, 0:64], float(EXPERTS - 1), None, ALU.min))
            link(vec.tensor_copy(metaf[:, 64:72], ps[0:1, 5, 0:8]))
            vec.tensor_copy(meta[:], metaf[:]).then_inc(r_ready, 1)
            vec.tensor_copy(dst[:], dstf[:]).then_inc(r_ready, 1)
            vec.wait_ge(r_exp, 2)
            mark(vec.tensor_reduce(gsum[:], gex[:], AX.X, ALU.add))
            link(vec.tensor_scalar(den[:], ex[:], 1.0, None, ALU.add))
            mark(vec.reciprocal(pg[:], gsum[:]))
            link(vec.reciprocal(g1[:], den[:]))
            link(vec.tensor_tensor(g1[:], g1[:], pg[:], ALU.mult))
            mark(vec.tensor_copy(wvec[:, 0, :], g1[:]))
            link(vec.tensor_tensor(wvec[:, 1, :], g1[:], ex[:], ALU.mult))

        @block2.tensor
        def _(pe):
            pe.wait_ge(r_ready, 3)
            for t in range(TILES):
                o = slice(t * EXPERTS, (t + 1) * EXPERTS)
                pe.matmul(ps[:, 0, o], cst3(C_LOW, P), both[:, t, :], start=True, stop=False)
                pe.matmul(ps[:, 0, o], ones[:], runs[:, t, :], start=False, stop=True)
            pe.matmul(ps[0:EXPERTS, 1, 0:1], runs[:, TILES, :], ones[:, 0:1], start=True, stop=True).then_inc(r_mm, 1)
            pe.wait_ge(r_ready, 4)
            pe.matmul(ps[:, 2, 0:EXPERTS], nbb[:], cst[0:EXPERTS, C_TRI32:C_TRI32 + EXPERTS], start=True, stop=True)
            pe.matmul(ps[0:EXPERTS, 3, 0:1], cst[0:EXPERTS, C_TRI32I:C_TRI32I + EXPERTS], nbc[:], start=True, stop=True)\
              .then_inc(r_mm, 1)
            pe.wait_ge(r_ready, 5)
            pe.matmul(ps[0:1, 4, 0:64], ones[0:EXPERTS, 0:1], bcmp[:], start=True, stop=True)
            pe.matmul(ps[0:1, 5, 0:8], nbc[:], ones[0:EXPERTS, 0:8], start=True, stop=True).then_inc(r_mm, 1)

        e_in = [sem(f"e_in{q}") for q in range(EP)]
        e_hi = sem("e_hi")
        e_lo = sem("e_lo")
        tix_in = sem("tix_in")
        pix_in = sem("pix_in")
        y_free = sem("y_free")
        pool_seen = sem("pool_seen")
        gx_in = sem("gx_in")
        gx_tr = sem("gx_tr")
        xT_hi = sem("xT_hi")
        xT_lo = sem("xT_lo")
        gate_up = sem("gate_up")
        e_silu = sem("e_silu")
        hid_v = sem("hid_v")
        hid_tr = sem("hid_tr")
        hidT_hi = sem("hidT_hi")
        hidT_lo = sem("hidT_lo")
        down = sem("down")
        y_act = sem("y_act")
        y_vec = sem("y_vec")
        y_st = sem("y_st")
        EW = 8
        part.close()
        block3 = part.enter_context(nc.Block())

        def blocks_of(eng):
            return eng.value_load(meta[0:1, 64:65], min_val=1, max_val=MAX_BLOCKS)

        @block3.sync
        def _(sp):
            nb = blocks_of(sp)

            def piece(e, q):
                return wexp[bass.ds(e, 1), q].rearrange("o p n -> p (o n)")

            e0 = sp.value_load(meta[0:1, 0:1], min_val=0, max_val=EXPERTS - 1)
            for q in range(2):
                sp.dma_start(est[q][:], piece(e0, q)).then_inc(e_in[q], 16)
            with sp.Fori(0, nb) as b:
                e = sp.value_load(meta[0:1, bass.ds(b, 1)], min_val=0, max_val=EXPERTS - 1)
                for q in range(2, EP):
                    rows = piece(e, q)
                    sp.wait_ge(e_lo, b * EP + (EW - EP + q + 1))
                    sp.dma_start(est[q][:], rows).then_inc(e_in[q], 16)
                e = sp.value_load(meta[0:1, bass.ds(b + 1, 1)], min_val=0, max_val=EXPERTS - 1)
                for q in range(2):
                    rows = piece(e, q)
                    sp.wait_ge(e_lo, b * EP + (EW + q + 1))
                    sp.dma_start(est[q][:], rows).then_inc(e_in[q], 16)

        @block3.gpsimd
        def _(pool):
            nb = blocks_of(pool)

            def gather(b):
                pool.dma_start(tix[:], list_dram[bass.ds(b * TB, TB)]).then_inc(tix_in, 16)
                pool.wait_ge(tix_in, b * 16 + 16)
                pool.sem_inc(pool_seen, 1)
                pool.indirect_dma_start(out=gX[:], out_offset=None, in_=h2_dram,
                                        in_offset=bass.IndirectOffsetOnAxis(ap=tix[:, 0:1], axis=0)).then_inc(gx_in, 16)

            pool.sem_inc(y_free, EW)
            gather(0)
            with pool.Fori(0, nb) as b:
                pool.wait_ge(gx_in, b * 16 + 16)
                pool.wait_ge(gx_tr, b + 1)
                gather(b + 1)
                pool.dma_start(pix[:], list_dram[bass.ds(b * TB, TB)]).then_inc(pix_in, 16)
                pool.wait_ge(pix_in, b * 16 + 16)
                pool.wait_ge(y_act, b + (EW + 1))
                pool.wait_ge(y_vec, b + (EW + 1))
                pool.sem_inc(pool_seen, 1)
                pool.indirect_dma_start(out=yb_dram, out_offset=bass.IndirectOffsetOnAxis(ap=pix[:, 1:2], axis=0),
                                        in_=yS[:], in_offset=None).then_inc(y_st, 16)
                pool.wait_ge(y_st, b * 16 + 16)
                pool.sem_inc(y_free, 1)
            pool.wait_ge(gx_in, nb * 16 + 16)

        @block3.scalar
        def _(act):
            nb = blocks_of(act)

            def hi(b, q):
                act.wait_ge(e_in[q], b * 16 + 16)
                act.wait_ge(gate_up if q < 4 else down, b + EW)
                act.activation(whi[q][:], est[q][:], ACT.Copy).then_inc(e_hi, 1)

            def x_hi(b):
                act.wait_ge(gx_tr, b + 1)
                act.wait_ge(gate_up, b + EW)
                for g in range(2):
                    act.activation(xT[0][:, 4 * g:4 * g + 4, :],
                                   ps[:, 2 + g, 0:4 * TB].rearrange("p (c t) -> p c t", c=4), ACT.Copy).then_inc(xT_hi, 1)

            act.sem_inc(y_act, EW)
            x_hi(0)
            hi(0, 0)
            hi(0, 1)
            with act.Fori(0, nb) as b:
                hi(b, 2)
                hi(b, 3)
                act.wait_ge(gate_up, b + (EW + 1))
                act.activation(sgate[:], ps[0:TB, 0, :], ACT.Silu).then_inc(e_silu, 1)
                hi(b, 4)
                act.wait_ge(hid_tr, b + 1)
                act.wait_ge(down, b + EW)
                act.activation(hidT[0][:], ps[:, 4, 0:EC * TB].rearrange("p (c t) -> p c t", c=EC), ACT.Copy)\
                   .then_inc(hidT_hi, 1)
                x_hi(b + 1)
                hi(b, 5)
                hi(b + 1, 0)
                hi(b + 1, 1)
                act.wait_ge(down, b + (EW + 1))
                act.wait_ge(y_free, b + EW)
                act.activation(yS[:, 0:512], ps[0:TB, 5, :], ACT.Copy).then_inc(y_act, 1)

        @block3.vector
        def _(vec):
            nb = blocks_of(vec)

            def lo(b, q):
                vec.wait_ge(e_hi, b * EP + (q + 1))
                vec.tensor_tensor(wlo[q][:], est[q][:], whi[q][:].bitcast(F32), ALU.subtract).then_inc(e_lo, 1)

            def x_lo(b):
                for g in range(2):
                    vec.wait_ge(xT_hi, b * 2 + (g + 1))
                    vec.tensor_tensor(xT[1][:, 4 * g:4 * g + 4, :],
                                      ps[:, 2 + g, 0:4 * TB].rearrange("p (c t) -> p c t", c=4),
                                      xT[0][:, 4 * g:4 * g + 4, :].bitcast(F32), ALU.subtract).then_inc(xT_lo, 1)

            for sm_ in (e_lo, y_vec):
                vec.sem_inc(sm_, EW)
            x_lo(0)
            lo(0, 0)
            lo(0, 1)
            with vec.Fori(0, nb) as b:
                lo(b, 2)
                lo(b, 3)
                vec.wait_ge(e_silu, b + 1)
                vec.tensor_tensor(hid[:], sgate[:], ps[0:TB, 1, :], ALU.mult).then_inc(hid_v, 1)
                lo(b, 4)
                vec.wait_ge(hidT_hi, b + 1)
                vec.tensor_tensor(hidT[1][:], ps[:, 4, 0:EC * TB].rearrange("p (c t) -> p c t", c=EC),
                                  hidT[0][:].bitcast(F32), ALU.subtract).then_inc(hidT_lo, 1)
                x_lo(b + 1)
                lo(b, 5)
                lo(b + 1, 0)
                lo(b + 1, 1)
                vec.wait_ge(down, b + (EW + 1))
                vec.wait_ge(y_free, b + EW)
                vec.tensor_copy(yS[:, 512:1024], ps[0:TB, 6, :]).then_inc(y_vec, 1)

        @block3.tensor
        def _(pe):
            nb = blocks_of(pe)

            def three(out, A, B, ka, kb, start, stop):
                pe.matmul(out, A[0][ka], B[0][kb], start=start, stop=False)
                pe.matmul(out, A[0][ka], B[1][kb], start=False, stop=False)
                return pe.matmul(out, A[1][ka], B[0][kb], start=False, stop=stop)

            A3 = slice(None)

            def x_transposes():
                for c in range(DC):
                    ins = pe.transpose(ps[:, 2 + c // 4, (c % 4) * TB:(c % 4 + 1) * TB], gX[:, c * P:(c + 1) * P],
                                       ident[0:TB, 0:TB])
                ins.then_inc(gx_tr, 1)

            pe.sem_inc(gate_up, EW)
            pe.sem_inc(down, EW)

            pe.wait_ge(gx_in, 16)
            x_transposes()
            with pe.Fori(0, nb) as b:
                pe.wait_ge(xT_lo, b * 2 + 2)
                for m in range(2):
                    for h in range(2):
                        q = 2 * m + h
                        pe.wait_ge(e_lo, b * EP + (EW + q + 1))
                        W = [w[q][:].rearrange("p (c n) -> p c n", n=DE) for w in (whi, wlo)]
                        for c in range(4):
                            ins = three(ps[0:TB, m, :], xT, W, (A3, 4 * h + c, A3), (A3, c, A3),
                                        h == 0 and c == 0, h == 1 and c == 3)
                ins.then_inc(gate_up, 1)
                pe.wait_ge(gx_in, b * 16 + 32)
                x_transposes()
                pe.wait_ge(hid_v, b + 1)
                for c in range(EC):
                    ins = pe.transpose(ps[:, 4, c * TB:(c + 1) * TB], hid[:, c * P:(c + 1) * P], ident[0:TB, 0:TB])
                ins.then_inc(hid_tr, 1)
                pe.wait_ge(hidT_lo, b + 1)
                pe.wait_ge(y_act, b + EW)
                pe.wait_ge(y_vec, b + EW)
                for h in range(2):
                    pe.wait_ge(e_lo, b * EP + (EW + 4 + h + 1))
                    W = [w[4 + h][:].rearrange("p (c n) -> p c n", n=D) for w in (whi, wlo)]
                    for c in range(2):
                        for n in range(2):
                            ins = three(ps[0:TB, 5 + n, :], hidT, W, (A3, 2 * h + c, A3),
                                        (A3, c, slice(n * 512, (n + 1) * 512)),
                                        h == 0 and c == 0, h == 1 and c == 1)
                ins.then_inc(down, 1)

        RING = 3
        c_x = [sem(f"c_x{i}") for i in range(RING)]
        c_y = [sem(f"c_y{i}") for i in range(RING)]
        c_zero = sem("c_zero")
        c_vec = sem("c_vec")
        c_add = sem("c_add")
        c_sum = sem("c_sum")
        c_pool = sem("c_pool")
        c_rstd = sem("c_rstd")
        c_out = sem("c_out")
        c_st = [sem(f"c_st{i}") for i in range(RING)]
        part.close()
        block4 = part.enter_context(nc.Block())

        @block4.sync
        def _(sp):
            for t in range(TILES):
                if t >= RING:
                    sp.wait_ge(c_out, t - RING + 1)
                sp.dma_start(cx[t % RING][:], x2_dram[t]).then_inc(c_x[t % RING], 16)
                rows = yb_dram[2 * P * t:2 * P * (t + 1)].rearrange("(p k) d -> p (k d)", k=2)
                if t == 0:
                    sp.wait_ge(c_zero, 1)
                    sp.dma_start(cy[0][0:DEC_SEQ, :], rows[0:DEC_SEQ]).then_inc(c_y[0], 16)
                    sp.dma_start(cy[0][FIRST_META:P, :], rows[FIRST_META:P]).then_inc(c_y[0], 16)
                else:
                    sp.dma_start(cy[t % RING][:], rows).then_inc(c_y[t % RING], 16)

        @block4.gpsimd
        def _(pool):
            for t in range(TILES):
                pool.wait_ge(c_sum, t + 1)
                pool.tensor_tensor(cq[:, TILES + t:TILES + t + 1], cq[:, t:t + 1], half[:, 3:4], ALU.add)\
                    .then_inc(c_pool, 1)
                pool.wait_ge(c_pool, t + 1)
                pool.tensor_tensor(cq[:, 2 * TILES + t:2 * TILES + t + 1], cq[:, TILES + t:TILES + t + 1], half[:, 0:1],
                                   ALU.pow).then_inc(c_rstd, 1)

        @block4.scalar
        def _(act):
            for t in range(TILES):
                act.wait_ge(c_add, t + 1)
                if t:
                    act.wait_ge(c_sum, t)
                act.activation(cscr[:], cx[t % RING][:], ACT.Square, accum_out=cq[:, t:t + 1]).then_inc(c_sum, 1)
                if t:
                    act.wait_ge(c_out, t)
                    act.dma_start(y_all[t - 1], co[(t - 1) % RING][:]).then_inc(c_st[(t - 1) % RING], 16)
            act.wait_ge(c_out, TILES)
            act.dma_start(y_all[TILES - 1], co[(TILES - 1) % RING][:]).then_inc(c_st[(TILES - 1) % RING], 16)
            for i in range(RING):
                act.wait_ge(c_st[i], 16 * (TILES // RING))

        @block4.vector
        def _(vec):
            def out(t):
                vec.wait_ge(c_rstd, t + 1)
                if t >= RING:
                    vec.wait_ge(c_st[t % RING], 16 * (t // RING))
                vec.scalar_tensor_tensor(co[t % RING][:], cx[t % RING][:], cq[:, 2 * TILES + t:2 * TILES + t + 1], gfin[:],
                                         ALU.mult, ALU.mult).then_inc(c_out, 1)

            vec.memset(cy[0][:], 0.0).then_inc(c_zero, 1)
            vec.tensor_scalar(gfin[:], gfin[:], float(D) ** 0.5, None, ALU.mult).then_inc(g_scaled, 1)
            vec.wait_ge(g_scaled, 4)
            for t in range(TILES):
                i = t % RING
                vec.wait_ge(c_x[i], 16 * (t // RING + 1))
                vec.wait_ge(c_y[i], 16 * (t // RING + 1 + (1 if i == 0 else 0)))
                vec.scalar_tensor_tensor(cx[i][:], cy[i][:, 0:D], wvec[:, 0, t:t + 1], cx[i][:], ALU.mult, ALU.add)\
                   .then_inc(c_vec, 1)
                vec.wait_ge(c_vec, t + 1)
                vec.scalar_tensor_tensor(cx[i][:], cy[i][:, D:2 * D], wvec[:, 1, t:t + 1], cx[i][:], ALU.mult, ALU.add)\
                   .then_inc(c_add, 1)
                if t:
                    out(t - 1)
            out(TILES - 1)

        part.close()


def lay_out(x_prompt, x_sample, state_ret, state_gla, meta_tokens, g_mix, w_in, w_gla_gk2, b_gla_gk, g_gla_norm,
            w_br_ret, w_br_gla, w_out, g_ffn, w_router_group, b_router_group, w_router_expert, b_router_expert,
            w_exp_gate, w_exp_up, w_exp_down, g_final):
    f = np.float32
    x_all = np.zeros((TILES + TPS, P, D), f)
    rows = x_all.reshape(-1, D)
    rows[0:DEC_SEQ] = x_sample[0]
    rows[FIRST_META:FIRST_META + N_META] = meta_tokens
    rows[DEC_SEQ + CHUNK:ROWS] = x_prompt[0]
    states = np.concatenate([state_ret[0, 0], state_gla[0, 0]]).transpose(1, 0, 2)
    RK, RV = HEADS * HK, HEADS * HV
    cuts = np.cumsum([0, RK, RK, RV, RV, RK, RK, RV, RV, RANK, D, D])
    w = w_in[0]
    part = [w[:, cuts[i]:cuts[i + 1]] for i in range(11)]

    def chunked(m):
        return m.reshape(-1, P, m.shape[1]).transpose(1, 0, 2).reshape(P, -1)

    def pieces(m):
        return list(m.reshape(P, -1, PIECE).transpose(1, 0, 2))

    low = np.zeros((D, P), f)
    low[:, 0:RANK] = part[8]
    out = pieces(chunked(low))
    for h in range(NHB):
        q, k, v, g = part[0:4] if h < HEADS else part[4:8]
        i = h % HEADS
        out += pieces(chunked(np.concatenate([q[:, i * HK:(i + 1) * HK], k[:, i * HK:(i + 1) * HK],
                                              v[:, i * HV:(i + 1) * HV], g[:, i * HV:(i + 1) * HV]], axis=1)))
    for d in range(DC):
        c = slice(d * P, (d + 1) * P)
        out += pieces(np.concatenate([chunked(part[9][:, c]), chunked(part[10][:, c]), chunked(w_br_ret[0][:, c]),
                                      chunked(w_br_gla[0][:, c])], axis=1))
    for c0, cn in OUT_COLS:
        out += pieces(chunked(w_out[0][:, c0:c0 + cn]))
    wmix = np.stack(out)
    E_ = EXPERTS
    gu = [x[0].reshape(E_, 2, 4, P, DE).transpose(0, 1, 3, 2, 4).reshape(E_, 2, P, EPC) for x in (w_exp_gate, w_exp_up)]
    dn = w_exp_down[0].reshape(E_, 2, 2, P, D).transpose(0, 1, 3, 2, 4).reshape(E_, 2, P, EPC)
    return {
        "x_all": x_all, "states": states, "consts": shape_constants(), "list_init": empty_list(), "g_mix": g_mix[0], "g_ffn": g_ffn[0],
        "g_final": g_final, "g_gla": g_gla_norm[0], "wmix": wmix,
        "gk2": np.concatenate([w_gla_gk2[0], b_gla_gk[0][None]]),
        "w_router": np.concatenate([w_router_expert[0], w_router_group[0]], axis=1).reshape(DC, P, 36).transpose(1, 0, 2),
        "b_router": np.concatenate([b_router_expert[0], b_router_group[0]]),
        "wexp": np.concatenate(gu + [dn], axis=1),
    }


OUTS = {"y_all": (TILES, P, D), "raw_out": (2 * SUPER, HK, HEADS, HV), "fin_out": (HK, NHB, HV)}


def kernel(**inputs):
    import concourse.bacc as bacc
    from concourse.bass_utils import run_bass_kernel_spmd

    arrays = {n: np.ascontiguousarray(a) for n, a in lay_out(**{n: np.asarray(a) for n, a in inputs.items()}).items()}
    nc = bacc.Bacc("TRN2", target_bir_lowering=False, num_devices=1)
    args = [nc.dram_tensor(n, a.shape, mybir.dt.from_np(a.dtype), kind="ExternalInput").ap() for n, a in arrays.items()]
    args += [nc.dram_tensor(n, s, F32, kind="ExternalOutput").ap() for n, s in OUTS.items()]
    build(nc, *args)
    got = run_bass_kernel_spmd(nc, [arrays], core_ids=[0]).results[0]
    y = np.asarray(got["y_all"]).reshape(ROWS, D)
    raw = np.asarray(got["raw_out"])[0:2].transpose(0, 2, 1, 3)
    fin = np.asarray(got["fin_out"]).transpose(1, 0, 2)

    def state(a):
        return np.ascontiguousarray(a)[None, None]

    return (y[None, DEC_SEQ + CHUNK:], y[None, 0:DEC_SEQ], state(fin[:HEADS]), state(fin[HEADS:]),
            state(raw[0]), state(raw[1]))
```

```python
from contextlib import ExitStack

import numpy as np

import concourse.bass as bass
from concourse import mybir

ALU = mybir.AluOpType
ACT = mybir.ActivationFunctionType
AX = mybir.AxisListType
F32 = mybir.dt.float32
F32R = mybir.dt.float32r
I32 = mybir.dt.int32
U32 = mybir.dt.uint32

P = 128
D = 1024
DC = D // P
CHUNK = 64
N_META = 16
SEQ = 1024
DEC_SEQ = 64
PAST_LEN = 128
HEADS = 4
HK = 64
HV = 128
RANK = 16
ROPE_BASE = 10000.0
EPS = 1e-6

ROWS = DEC_SEQ + CHUNK + SEQ
FIRST_META = DEC_SEQ + CHUNK - N_META
TILES = ROWS // P
TPS = 3
SUPER = TILES // TPS
TOK = TPS * P
NHB = 2 * HEADS
HW = 2 * HK + 2 * HV
ITEMS = NHB * TPS
RET_ITEMS = HEADS * TPS

PIECE = 1024
OUT_COLS = [(0, 384), (384, 384), (768, 256)]
PIECES = [1] + [3] * NHB + [3] * DC + [3, 3, 2]
BLOCKS = len(PIECES)
PIECE0 = [sum(PIECES[:w]) for w in range(BLOCKS)]
NP_SB = sum(PIECES)
STAGE = 3
W_HEAD, W_Z, W_OUT = 1, 1 + NHB, 1 + NHB + DC

GROUPS = 4
PER_GROUP = 8
EXPERTS = GROUPS * PER_GROUP
DE = 512
EC = DE // P
TB = 96
PAIRS = 2 * (N_META + SEQ + DEC_SEQ)
MAX_BLOCKS = PAIRS // TB + EXPERTS
MAX_PER_EXPERT = -(-(PAIRS // 2) // TB)
LIST = (MAX_BLOCKS + 1) * TB
DUMP = LIST
EP = 6
EPC = 2048
BIG = 1e30

SEED = 4

C_IDENT, C_DMAT, C_TRI, C_LOW = 0, 128, 128 + HEADS * 128, 256 + HEADS * 128
C_KDEC = C_LOW + 128
C_QDEC = C_KDEC + 2 * HEADS
C_IND = C_QDEC + HEADS
C_VALID = C_IND + 2
C_DUMP = C_VALID + TILES
C_TOKID = C_DUMP + 2 * TILES
C_IOTA = C_TOKID + TILES
C_GRP = C_IOTA + EXPERTS
C_STEP = C_GRP + EXPERTS
C_TRI32 = C_STEP + MAX_PER_EXPERT
C_TRI32I = C_TRI32 + EXPERTS
C_IOTAB = C_TRI32I + EXPERTS
C_ROT = C_IOTAB + 64
ROT = 3 * (HK // 2)
C_END = C_ROT + TILES * ROT


def shape_constants():
    c = np.zeros((P, C_END), np.float32)
    r = np.arange(P)
    same = (r[:, None] // CHUNK) == (r[None, :] // CHUNK)
    c[:, C_IDENT:C_IDENT + P] = np.eye(P)
    log_g = np.log1p(-np.exp2(-5.0 - np.arange(HEADS)))
    idx = r % CHUNK
    for h in range(HEADS):
        c[:, C_DMAT + h * P:C_DMAT + (h + 1) * P] = np.where(
            same, np.exp(np.abs(idx[:, None] - idx[None, :]) * log_g[h]), 0) * HK ** -0.5
        for k in range(2):
            c[:, C_KDEC + k * HEADS + h] = np.exp((CHUNK - 1.0 - idx) * log_g[h]) * HK ** -0.5 * (r // CHUNK == k)
        c[:, C_QDEC + h] = np.exp((idx + 1.0) * log_g[h])
    c[:, C_TRI:C_TRI + P] = same & (r[:, None] > r[None, :])
    c[:, C_LOW:C_LOW + P] = r[:, None] < r[None, :]
    c[:CHUNK, C_IND] = 1
    c[CHUNK:, C_IND + 1] = 1
    row = np.arange(TILES)[None, :] * P + r[:, None]
    valid = (row < DEC_SEQ) | (row >= FIRST_META)
    c[:, C_VALID:C_VALID + TILES] = valid
    for k in range(2):
        c[:, C_DUMP + k * TILES:C_DUMP + (k + 1) * TILES] = np.where(valid, 0, DUMP + 2 * r[:, None] + k)
    c[:, C_TOKID:C_TOKID + TILES] = row
    c[:, C_IOTA:C_IOTA + EXPERTS] = np.arange(EXPERTS)
    c[:, C_GRP:C_GRP + EXPERTS] = np.arange(EXPERTS) // PER_GROUP
    c[:, C_STEP:C_STEP + MAX_PER_EXPERT] = np.arange(MAX_PER_EXPERT) * TB
    e = np.arange(EXPERTS)
    c[:EXPERTS, C_TRI32:C_TRI32 + EXPERTS] = (e[:, None] < e[None, :]) * float(TB)
    c[:EXPERTS, C_TRI32I:C_TRI32I + EXPERTS] = e[:, None] <= e[None, :]
    c[:, C_IOTAB:C_IOTAB + 64] = np.arange(64)
    pos = np.where(row < DEC_SEQ, PAST_LEN + row, row - DEC_SEQ - CHUNK).astype(np.float32)
    inv = (ROPE_BASE ** (-2.0 * np.arange(HK // 2) / HK)).astype(np.float32)
    ang = (pos[:, :, None] * inv).astype(np.float64)
    rot = np.concatenate([np.cos(ang), -np.sin(ang), np.sin(ang)], axis=-1)
    c[:, C_ROT:] = rot.reshape(P, TILES * ROT)
    return c


def empty_list():
    s = np.zeros((LIST + 2 * P, 3), np.int32)
    s[:, 1] = ROWS + np.arange(LIST + 2 * P) % TB
    return s


def build(nc, x_all, states, consts, list_init, g_mix, g_ffn, g_final, g_gla, wmix, gk2, w_router, b_router, wexp,
          y_all, raw_out, fin_out):
    x2_dram = nc.dram_tensor("x2_scratch", (ROWS + TB, D), F32).ap()
    h2_dram = nc.dram_tensor("h2_scratch", (ROWS, D), F32).ap()
    list_dram = nc.dram_tensor("pair_list", (LIST + 2 * P, 3), I32).ap()

    with ExitStack() as ctx:
        arena = ctx.enter_context(nc.sbuf_tensor("arena", [P, (229344 - 16512) // 4], F32))
        base = 16512
        limit = 229344
        place = [base]

        def at(name, shape, dt=F32):
            size = 4 * int(np.prod(shape[1:]))
            t = nc.alloc_sbuf_tensor_at(name, list(shape), dt, offset=place[0])
            place[0] += -(-size // 32) * 32
            assert place[0] <= limit, (name, place[0])
            return t

        def sem(name):
            return ctx.enter_context(nc.semaphore(name))

        cst = at("cst", [P, C_END])
        logits = at("logits", [P, TILES, 40])
        half = at("half", [P, 4])
        keep_base = place[0]

        hT = [at(f"hT{i}", [P, DC, TOK], F32R) for i in range(2)]
        oT_at = place[0]
        oT = [at(f"oT{i}", [P, NHB, TOK], F32R) for i in range(2)]
        oT_end = place[0]
        h2T = at("h2T", [P, TPS * D])
        place[0] = oT_end
        mT = [at(f"mT{i}", [P, DC, TOK], F32R) for i in range(2)]
        stage = [at(f"stage{i}", [P, PIECE]) for i in range(STAGE)]
        whl = [[at(f"w{i}{j}", [P, 3 * PIECE], F32R) for j in range(2)] for i in range(2)]
        h_at = place[0]
        H = [at(f"H{j}", [P, D]) for j in range(TPS)]
        XR = [at(f"XR{j}", [P, D]) for j in range(TPS)]
        gmix = at("gmix", [P, D])
        gffn = at("gffn", [P, D])
        ggla = at("ggla", [P, HV])
        gk2s = at("gk2s", [RANK + 1, HEADS * HK])
        glrT = at("glrT", [32, TOK])
        wr = at("wr", [P, DC, EXPERTS + GROUPS])
        rb = at("rb", [P, EXPERTS + GROUPS])
        S0 = at("S0", [HK, NHB, HV])
        RAW = at("RAW", [HK, HEADS, HV])
        SW = at("SW", [HK, 4, 2, HV])
        keep = at("keep", [HK, 1])
        pS = at("pS", [P, 4, HW])
        qk = at("qk", [P, 2, 2 * HK])
        rt = at("rt", [P, 2 * HK])
        kd = at("kd", [P, 2, 2, HK])
        qkT = at("qkT", [HK, 4 * P])
        sT = at("sT", [P, P])
        og = at("og", [P, 2, HV])
        sq = rt[:]
        st6 = at("st6", [P, 2, 6])
        mv = at("mv", [P, 2, 2])
        ve = at("ve", [P, 2])
        rs = at("rs", [P, 2])
        z_at = place[0]
        la = at("la", [P, TPS, HEADS * HK])
        place[0] = z_at
        sz = at("sz", [P, 2, TOK])
        z_at = place[0]
        edec = at("edec", [P, TPS, HEADS * HK])
        ob = at("ob", [P, HV])
        tb = at("tb", [P, 2, HV])
        z_end = place[0]
        place[0] = z_at
        mz = at("mz", [P, 3, TOK])
        assert place[0] <= z_end
        place[0] = z_end
        ga = edec
        aT = at("aT", [HK, HEADS, 2 * TPS])
        ssq = at("ssq", [P, 8])
        vn = at("vn", [P, 8])
        rn = at("rn", [P, 8])

        scr = mz[:, :, :].rearrange("p a b -> p (a b)")[:, 0:D]

        place[0] = keep_base
        est = [at(f"est{i}", [P, EPC]) for i in range(EP)]
        assert place[0] <= oT_end
        place[0] = oT_end
        whi = [at(f"whi{i}", [P, EPC], F32R) for i in range(EP)]
        wlo = [at(f"wlo{i}", [P, EPC], F32R) for i in range(EP)]
        gX = at("gX", [TB, D])
        xT = [at(f"xT{i}", [P, DC, TB], F32R) for i in range(2)]
        sgate = at("sgate", [TB, DE])
        hid = at("hid", [TB, DE])
        hidT = [at(f"hidT{i}", [P, EC, TB], F32R) for i in range(2)]
        yS = at("yS", [TB, D])
        tix = at("tix", [TB, 3], I32)
        pix = at("pix", [TB, 3], I32)
        gfin = at("gfin", [P, D])

        dst = at("dst", [P, 2, TILES], I32)

        meta = at("meta", [1, 72], I32)
        moe_end = place[0]
        place[0] = oT_end + 4 * EPC * (EP + 1)

        gm8 = at("gm8", [P, TILES, 8])
        gi8 = at("gi8", [P, TILES, 8], U32)
        gif = at("gif", [P, TILES])
        gmask = at("gmask", [P, TILES, EXPERTS])
        pen = at("pen", [P, TILES, EXPERTS])
        lm = at("lm", [P, TILES, EXPERTS])
        em8 = at("em8", [P, TILES, 8])
        ei8 = at("ei8", [P, TILES, 8], U32)
        eif = at("eif", [P, TILES, 2])
        ngm = at("ngm", [P, TILES, GROUPS])
        gex = at("gex", [P, TILES, GROUPS])
        gsum = at("gsum", [P, TILES])
        pg = at("pg", [P, TILES])
        dd = at("dd", [P, TILES])
        ex = at("ex", [P, TILES])
        den = at("den", [P, TILES])
        g1 = at("g1", [P, TILES])
        g2 = at("g2", [P, TILES])
        oh = [at(f"oh{k}", [P, TILES, EXPERTS]) for k in range(2)]
        both = at("both", [P, TILES, EXPERTS])
        runs = at("runs", [P, TILES + 1, EXPERTS])
        ones = at("ones", [P, P])
        cntc = at("cntc", [EXPERTS, 1])
        cmp = at("cmp", [EXPERTS, MAX_PER_EXPERT])
        nbc = at("nbc", [EXPERTS, 1])
        nbb = at("nbb", [EXPERTS, P])
        bend = at("bend", [EXPERTS, 1])
        bcmp = at("bcmp", [EXPERTS, 64])
        pstart = at("pstart", [P, EXPERTS])
        rank = at("rank", [P, TILES, EXPERTS])
        pick = at("pick", [P, TILES, EXPERTS])
        dstf = at("dstf", [P, 2, TILES])
        tokid = at("tokid", [P, TILES, 2, 3], I32)
        metaf = at("metaf", [1, 72])
        assert place[0] <= h_at
        assert place[0] <= oT_end + 4 * 2 * EP * EPC
        place[0] = moe_end
        place[0] = keep_base
        cx = [at(f"cx{i}", [P, D]) for i in range(TILES)]
        co = [at(f"co{i}", [P, D]) for i in range(TILES)]
        cq = at("cq", [P, 3 * TILES])
        cscr = at("cscr", [P, D])
        assert place[0] <= oT_end + 4 * 2 * EP * EPC
        ps = ctx.enter_context(nc.psum_tensor("ps", [P, 8, 512], F32))

        ident = cst[:, C_IDENT:C_IDENT + P]
        GB = [6, 2, 4]

        cst_in = sem("cst_in")
        par_in = sem("par_in")
        ones_set = sem("ones_set")
        g_scaled = sem("g_scaled")
        x_in = [sem(f"x_in{j}") for j in range(TPS)]
        xr_in = [sem(f"xr_in{j}") for j in range(TPS)]
        w_in = [sem(f"w_in{i}") for i in range(STAGE)]
        w_hi = sem("w_hi")
        w_lo = sem("w_lo")
        vec_step = sem("vec_step")
        pool_step = sem("pool_step")
        n1_sum = sem("n1_sum")
        n1_rstd = sem("n1_rstd")
        n1_h = sem("n1_h")
        n1_tr = sem("n1_tr")
        hT_hi = sem("hT_hi")
        hT_lo = sem("hT_lo")
        glr_mm = sem("glr_mm")
        glr_cp = sem("glr_cp")
        gate_mm = sem("gate_mm")
        gate_cp = sem("gate_cp")
        gate_l = sem("gate_l")
        gate_la = sem("gate_la")
        dec_mm = sem("dec_mm")
        dec_e = sem("dec_e")
        proj = sem("proj")
        p_cp = sem("p_cp")
        silu = sem("silu")
        rot = sem("rot")
        kd_done = sem("kd_done")
        sgn_pool = sem("sgn_pool")
        tr_u = sem("tr_u")
        qkT_cp = sem("qkT_cp")
        s_upd = sem("s_upd")
        score = sem("score")
        sT_cp = sem("sT_cp")
        o_mm = sem("o_mm")
        pe_seen = sem("pe_seen")
        stat = sem("stat")
        t_vec = sem("t_vec")
        rstd = sem("rstd")
        og_act = sem("og_act")
        o_tr = sem("o_tr")
        oT_hi = sem("oT_hi")
        oT_lo = sem("oT_lo")
        zr_mm = sem("zr_mm")
        br_mm = sem("br_mm")
        z_sig = sem("z_sig")
        m_part = sem("m_part")
        m_sum = sem("m_sum")
        mT_hi = sem("mT_hi")
        mT_lo = sem("mT_lo")
        out_mm = sem("out_mm")
        x2_add = sem("x2_add")
        n2_sum = sem("n2_sum")
        n2_rstd = sem("n2_rstd")
        n2_h = sem("n2_h")
        n2_tr = sem("n2_tr")
        n2_cp = sem("n2_cp")
        log_mm = sem("log_mm")
        log_add = sem("log_add")
        x2_st = [sem(f"x2_st{j}") for j in range(TPS)]
        h2_st = [sem(f"h2_st{j}") for j in range(TPS)]
        raw_st = sem("raw_st")
        l_init = sem("l_init")
        x2_pad = sem("x2_pad")
        fin_st = sem("fin_st")

        cst3 = lambda c, n: cst[:, c:c + n]

        part = ExitStack()
        block = part.enter_context(nc.Block())

        def tot(s, per, n):
            return s * per + (SEED + n)

        V = slice(2 * HK, 2 * HK + HV)
        G = slice(2 * HK + HV, HW)
        B_T, B_U, B_S, B_O, B_OT, B_G = 2, 3, 4, 5, 6, 7

        def qT(k, c0, c1):
            o = (k % 2) * 2 * P if k < RET_ITEMS else (k % 4) * P
            return qkT[:, o + c0:o + c1]

        def used(s, w):
            if w < 0:
                return out_mm, s * (3 * TPS) + (SEED + (w + 1) * TPS)
            if w < W_HEAD:
                return glr_mm, s + (SEED + 1)
            if w < W_Z:
                return proj, s * ITEMS + (SEED + (w - W_HEAD + 1) * TPS)
            if w < W_OUT:
                return br_mm, s * DC + (w - W_Z + 1)
            return out_mm, s * (3 * TPS) + (SEED + (w - W_OUT + 1) * TPS)

        @block.sync
        def _(sp):
            AHEAD = PIECE0[W_HEAD + 1]
            sp.dma_start(H[0][:], x_all[0]).then_inc(x_in[0], 16)
            sp.dma_start(gmix[:], g_mix.partition_broadcast(P)).then_inc(cst_in, 16)
            sp.dma_start(cst[:], consts).then_inc(cst_in, 16)
            for j in range(1, TPS):
                sp.dma_start(H[j][:], x_all[j]).then_inc(x_in[j], 16)
            for r in range(STAGE):
                sp.dma_start(stage[r][:], wmix[r]).then_inc(w_in[r], 16)
            for dst_, src_ in ((S0[:], states), (gk2s[:], gk2), (ggla[:], g_gla.partition_broadcast(P)),
                               (gffn[:], g_ffn.partition_broadcast(P)), (rb[:], b_router.partition_broadcast(P)),
                               (wr[:], w_router)):
                sp.dma_start(dst_, src_).then_inc(par_in, 16)
            sp.dma_start(list_dram, list_init).then_inc(l_init, 16)
            sp.dma_start(x2_dram[ROWS:ROWS + TB], x_all[TILES][0:TB]).then_inc(x2_pad, 16)
            for r in range(STAGE, AHEAD):
                sp.wait_ge(w_lo, SEED + r - STAGE + 1)
                sp.dma_start(stage[r % STAGE][:], wmix[r]).then_inc(w_in[r % STAGE], 16)
            with sp.Fori(0, SUPER) as s:
                for r in range(AHEAD, NP_SB + AHEAD):
                    if r == PIECE0[W_Z]:
                        sp.wait_ge(n2_h, s * TPS + SEED)
                        for j in range(TPS):
                            rows = x_all[bass.ds(s * TPS + j, 1)].rearrange("o p d -> p (o d)")
                            sp.wait_ge(x2_st[j], s * 16 + 16)
                            sp.dma_start(XR[j][:], rows).then_inc(xr_in[j], 16)
                        sp.wait_ge(n1_tr, tot(s, TPS, TPS))
                        sp.wait_ge(n2_tr, s * TPS + SEED)
                        for j in range(TPS):
                            rows = x_all[bass.ds(s * TPS + (TPS + j), 1)].rearrange("o p d -> p (o d)")
                            sp.wait_ge(h2_st[j], s * 16 + 16)
                            sp.dma_start(H[j][:], rows).then_inc(x_in[j], 16)
                    sp.wait_ge(w_lo, s * NP_SB + (SEED + r - STAGE + 1))
                    sp.dma_start(stage[r % STAGE][:], wmix[r % NP_SB]).then_inc(w_in[r % STAGE], 16)
            sp.wait_ge(s_upd, SUPER * ITEMS + SEED)
            sp.dma_start(fin_out, S0[:]).then_inc(fin_st, 16)
            sp.wait_ge(fin_st, 16)
            sp.wait_ge(raw_st, 16 * (2 * SUPER + 1))


        @block.scalar
        def _(act):
            def rms_sum(j, s_, first):
                act.wait_ge(x_in[j], s_ * 16 + 16)
                if not first:
                    act.wait_ge(n1_sum, s_ * TPS + j)
                    act.wait_ge(n2_sum, (s_ - 1) * TPS + SEED)
                elif j:
                    act.wait_ge(n1_sum, j)
                act.activation(scr, H[j][:], ACT.Square, accum_out=ssq[:, j:j + 1]).then_inc(n1_sum, 1)

            def hT_evac(j, s_):
                for g in range(2):
                    if g == 0:
                        act.wait_ge(n1_tr, tot(s_, TPS, j + 1))
                    act.activation(hT[0][:, 4 * g:4 * g + 4, j * P:(j + 1) * P],
                                   ps[:, GB[j] + g, :].rearrange("p (c t) -> p c t", c=4), ACT.Copy)\
                       .then_inc(hT_hi, 1)

            def split_hi(w, s):
                for q in range(PIECES[w]):
                    r = PIECE0[w] + q
                    act.wait_ge(w_in[r % STAGE], s * (16 * (NP_SB // STAGE)) + 16 * (r // STAGE + 1))
                    if q == 0:
                        act.wait_ge(*used(s, w - 2))
                    act.activation(whl[w % 2][0][:, q * PIECE:(q + 1) * PIECE], stage[r % STAGE][:], ACT.Copy)\
                       .then_inc(w_hi, 1)
                    yield


            for k_, sm_ in ((SEED, p_cp), (SEED, silu), (SEED, qkT_cp), (SEED, z_sig), (SEED, og_act), (SEED, n2_sum),
                            (SEED, oT_hi), (SEED, mT_hi), (SEED, w_hi), (SEED, hT_hi), (SEED, gate_cp), (SEED, gate_l), (SEED, dec_e)):
                act.sem_inc(sm_, k_)
            for j in range(TPS):
                rms_sum(j, 0, True)
            for j in range(TPS):
                hT_evac(j, 0)
            for w in (0, 1):
                for _ in split_hi(w, 0):
                    pass
            with act.Fori(0, SUPER) as s:
                splits = split_hi(W_HEAD + 1, s)
                next(splits)
                for i in range(ITEMS + 5):
                    if i < ITEMS:
                        act.wait_ge(proj, tot(s, ITEMS, i + 1))
                        act.wait_ge(o_mm, s * ITEMS + (SEED + i - 3))
                        act.wait_ge(t_vec, s * ITEMS + (SEED + i - 3))
                        act.activation(pS[:, i % 4, :], ps[:, i % 2, 0:HW], ACT.Copy).then_inc(p_cp, 1)
                        act.wait_ge(p_cp, tot(s, ITEMS, i + 1))
                        act.activation(pS[:, i % 4, G], pS[:, i % 4, G], ACT.Silu).then_inc(silu, 1)
                    if 1 <= i <= ITEMS:
                        k = i - 1
                        act.wait_ge(tr_u, tot(s, ITEMS, k + 1))
                        n = 2 * P if k < RET_ITEMS else P
                        free = k - 1 if k < RET_ITEMS else max(k - 3, RET_ITEMS - 1 + (k - RET_ITEMS) // 2)
                        act.wait_ge(o_mm, s * ITEMS + (SEED + free))
                        act.activation(qT(k, 0, n), ps[0:HK, B_T, 0:n], ACT.Copy,
                                       scale=1.0 if k < RET_ITEMS else HK ** -0.5).then_inc(qkT_cp, 1)
                    if 4 <= i <= ITEMS + 3:
                        k = i - 4
                        act.wait_ge(t_vec, tot(s, ITEMS, k + 1))
                        act.wait_ge(rstd, tot(s, ITEMS, k + 1))
                        act.wait_ge(o_tr, s * ITEMS + (SEED + k - 1))
                        act.activation(og[:, k % 2, :], tb[:, k % 2, :], ACT.Copy, scale=rs[:, k % 2:k % 2 + 1])\
                           .then_inc(og_act, 1)
                    if RET_ITEMS + 3 <= i <= ITEMS + 2:
                        k = i - 3
                        act.wait_ge(o_mm, tot(s, ITEMS, k + 1))
                        act.wait_ge(stat, s * ITEMS + k)
                        act.activation(sq, ps[:, B_O, 0:HV], ACT.Square,
                                       accum_out=mv[:, k % 2, 1:2]).then_inc(stat, 1)
                    if i in (RET_ITEMS - 1, ITEMS - 1):
                        m = 0 if i < RET_ITEMS else 1
                        act.wait_ge(s_upd, tot(s, ITEMS, i - 1))
                        act.dma_start(raw_out[bass.ds(s * 2 + m, 1)].rearrange("o k h v -> k (o h v)"),
                                      RAW[:, :, :].rearrange("k h v -> k (h v)")).then_inc(raw_st, 16)
                    if i >= 5:
                        k = i - 5
                        act.wait_ge(o_tr, tot(s, ITEMS, k + 1))
                        act.activation(oT[0][:, k // TPS, (k % TPS) * P:(k % TPS + 1) * P],
                                       ps[:, B_OT, 0:P], ACT.Copy).then_inc(oT_hi, 1)
                    if i == 0:
                        act.wait_ge(glr_mm, s + (SEED + 1))
                        act.activation(glrT[0:RANK, :], ps[0:RANK, B_G, 0:TOK], ACT.Copy).then_inc(glr_cp, 1)
                    if i == 1:
                        act.wait_ge(gate_mm, s * 2 + (SEED + 1))
                        act.activation(la[:, 0:2, :].rearrange("p t n -> p (t n)"), ps[:, B_G, :], ACT.Copy)\
                           .then_inc(gate_cp, 1)
                    if i == 2:
                        act.wait_ge(gate_mm, s * 2 + (SEED + 2))
                        act.activation(la[:, 2, :], ps[:, B_G, 0:256], ACT.Copy).then_inc(gate_cp, 1)
                        act.wait_ge(gate_cp, s * 2 + (SEED + 2))
                        laf, gaf = (x[:, :, :].rearrange("p t n -> p (t n)") for x in (la, ga))
                        act.activation(gaf, laf, ACT.Abs).then_inc(gate_l, 1)
                        act.wait_ge(gate_l, s * 3 + (SEED + 1))
                        act.activation(gaf, gaf, ACT.Exp, scale=-1.0).then_inc(gate_l, 1)
                        act.wait_ge(gate_l, s * 3 + (SEED + 2))
                        act.activation(gaf, gaf, ACT.Ln, bias=1.0).then_inc(gate_l, 1)
                    if i == 5:
                        act.wait_ge(dec_mm, s * 2 + (SEED + 1))
                        act.activation(edec[:, 0:2, :].rearrange("p t n -> p (t n)"), ps[:, B_G, :], ACT.Exp)\
                           .then_inc(dec_e, 1)
                    if i == 6:
                        act.wait_ge(dec_mm, s * 2 + (SEED + 2))
                        act.activation(edec[:, 2, :], ps[:, B_G, 0:256], ACT.Exp).then_inc(dec_e, 1)
                        act.activation(aT[:, :, :].rearrange("p h c -> p (h c)"),
                                       ps[0:HK, B_G, 256:256 + HEADS * 2 * TPS], ACT.Exp).then_inc(dec_e, 1)
                    if i % TPS == TPS - 1 and i + 1 < ITEMS:
                        splits = split_hi(W_HEAD + (i + 1) // TPS + 1, s)
                    next(splits, None)
                act.wait_ge(log_mm, s * TPS + SEED)
                def mt_evac(d):
                    act.wait_ge(m_sum, tot(s, DC, d + 1))
                    act.activation(mT[0][:, d, :], mz[:, 2, :], ACT.Copy).then_inc(mT_hi, 1)
                for d in range(DC):
                    w = W_Z + d
                    b0 = [(0, 1, 6, 7), (2, 3, 4, 5)][d % 2]
                    for _ in split_hi(w + 1, s):
                        pass
                    if d:
                        mt_evac(d - 1)
                    act.wait_ge(m_part, s * DC + (SEED + d))
                    act.wait_ge(zr_mm, s * 2 * DC + (SEED + 2 * d + 1))
                    act.activation(sz[:, 0, :], ps[:, b0[0], 0:TOK], ACT.Sigmoid)
                    act.wait_ge(zr_mm, s * 2 * DC + (SEED + 2 * d + 2))
                    act.activation(sz[:, 1, :], ps[:, b0[1], 0:TOK], ACT.Sigmoid).then_inc(z_sig, 1)
                mt_evac(DC - 1)
                for _ in split_hi(W_OUT + 1, s):
                    pass
                act.wait_ge(mT_lo, tot(s, DC, DC))
                for j in range(TPS):
                    rms_sum(j, s + 1, False)
                for _ in split_hi(W_OUT + 2, s):
                    pass
                for _ in split_hi(0, s + 1):
                    pass
                for j in range(TPS):
                    act.wait_ge(x2_add, s * 3 * TPS + (SEED + 2 * TPS + j + 1))
                    act.wait_ge(n1_sum, s * TPS + 2 * TPS)
                    act.wait_ge(n2_sum, tot(s, TPS, j))
                    act.activation(scr, XR[j][:], ACT.Square, accum_out=ssq[:, 3 + j:4 + j]).then_inc(n2_sum, 1)
                for j in range(TPS):
                    hT_evac(j, s + 1)
                for _ in split_hi(1, s + 1):
                    pass
                act.wait_ge(out_mm, tot(s, 3 * TPS, 3 * TPS))
                for j in range(TPS):
                    act.wait_ge(n2_tr, tot(s, TPS, j + 1))
                    act.activation(h2T[:, j * D:(j + 1) * D],
                                   ps[:, GB[j]:GB[j] + 2, :].rearrange("p b n -> p (b n)"), ACT.Copy).then_inc(n2_cp, 1)
                for j in range(TPS):
                    act.dma_start(x2_dram[bass.ds((s * TPS + j) * P, P)], XR[j][:])\
                       .then_inc(x2_st[j], 16)
                    act.dma_start(h2_dram[bass.ds((s * TPS + j) * P, P)], H[j][:]).then_inc(h2_st[j], 16)

        @block.gpsimd
        def _(pool):
            def rms(j, col, total, out_sem, in_sem, value):
                pool.wait_ge(in_sem, value)
                pool.tensor_tensor(vn[:, col:col + 1], ssq[:, col:col + 1], half[:, 3:4], ALU.add)\
                    .then_inc(pool_step, 1)
                step[0] += 1
                pool.wait_ge(pool_step, step[0])
                pool.tensor_tensor(rn[:, col:col + 1], vn[:, col:col + 1], half[:, 0:1], ALU.pow).then_inc(out_sem, 1)

            step = [0]
            pool.memset(half[:, 0:1], -0.5).then_inc(pool_step, 1)
            for f, value in enumerate((EPS, EPS * HV, EPS * D)):
                pool.memset(half[:, f + 1:f + 2], value).then_inc(pool_step, 1)
            pool.memset(kd[:], 0.0).then_inc(pool_step, 1)
            pool.wait_ge(pool_step, 5)
            step[0] = 5
            for sm_ in (kd_done, sgn_pool, rstd, m_sum, n2_rstd):
                pool.sem_inc(sm_, SEED)
            for j in range(TPS):
                rms(j, j, None, n1_rstd, n1_sum, j + 1)
            pool.wait_ge(g_scaled, 3)
            with pool.Fori(0, SUPER) as s:
                pool.sem_clear(pool_step)
                step[0] = 0
                for i in range(ITEMS + 4):

                    if i < ITEMS:
                        h = i // TPS
                        if i < RET_ITEMS:
                            pool.wait_ge(tr_u, s * ITEMS + (SEED + i - 1))
                            pool.wait_ge(rot, s * RET_ITEMS + (SEED + i + 1))
                            for c in range(2):
                                f = C_KDEC + c * HEADS + h
                                ins = pool.tensor_tensor(kd[:, i % 2, c, :], qk[:, i % 2, HK:2 * HK],
                                                         cst[:, f:f + 1].to_broadcast([P, HK]), ALU.mult)
                            ins.then_inc(kd_done, 1)
                        else:
                            pool.wait_ge(silu, tot(s, ITEMS, i + 1))
                            pool.tensor_tensor(pS[:, i % 4, G], pS[:, i % 4, G], ggla[:], ALU.mult).then_inc(sgn_pool, 1)
                    if 3 <= i <= ITEMS + 2:
                        k = i - 3
                        pool.wait_ge(stat, s * ITEMS + (k + 1))
                        pool.wait_ge(og_act, s * ITEMS + (SEED + k - 1))
                        f = 1 if k < RET_ITEMS else 2
                        pool.tensor_tensor(ve[:, k % 2:k % 2 + 1], mv[:, k % 2, 1:2], half[:, f:f + 1], ALU.add)\
                            .then_inc(pool_step, 1)
                        step[0] += 1
                        pool.wait_ge(pool_step, step[0])
                        pool.tensor_tensor(rs[:, k % 2:k % 2 + 1], ve[:, k % 2:k % 2 + 1], half[:, 0:1], ALU.pow)\
                            .then_inc(rstd, 1)
                for d in range(DC):
                    pool.wait_ge(m_part, tot(s, DC, d + 1))
                    pool.wait_ge(mT_lo, s * DC + (SEED + d))
                    pool.tensor_tensor(mz[:, 2, :], mz[:, 0, :], mz[:, 1, :], ALU.add).then_inc(m_sum, 1)
                for j in range(TPS):
                    rms(j, j, None, n1_rstd, n1_sum, s * TPS + (TPS + j + 1))
                for j in range(TPS):
                    rms(j, 3 + j, None, n2_rstd, n2_sum, tot(s, TPS, j + 1))


        @block.vector
        def _(vec):
            step = [0]

            def mark(ins):
                step[0] += 1
                ins.then_inc(vec_step, 1)
                return step[0]

            def norm1(j, s_):
                vec.wait_ge(n1_rstd, s_ * TPS + (j + 1))
                vec.scalar_tensor_tensor(H[j][:], H[j][:], rn[:, j:j + 1], gmix[:], ALU.mult, ALU.mult)\
                   .then_inc(n1_h, 1)

            def hT_lo_part(j, s_):
                for g in range(2):
                    vec.wait_ge(hT_hi, s_ * (2 * TPS) + (SEED + 2 * j + g + 1))
                    o = (slice(None), slice(4 * g, 4 * g + 4), slice(j * P, (j + 1) * P))
                    vec.tensor_tensor(hT[1][o], ps[:, GB[j] + g, :].rearrange("p (c t) -> p c t", c=4),
                                      hT[0][o].bitcast(F32), ALU.subtract).then_inc(hT_lo, 1)

            def split_lo(w, s):
                for q in range(PIECES[w]):
                    r = PIECE0[w] + q
                    vec.wait_ge(w_hi, s * NP_SB + (SEED + r + 1))
                    o = (slice(None), slice(q * PIECE, (q + 1) * PIECE))
                    vec.tensor_tensor(whl[w % 2][1][o], stage[r % STAGE][:], whl[w % 2][0][o].bitcast(F32),
                                      ALU.subtract).then_inc(w_lo, 1)
                    yield

            vec.wait_ge(cst_in, 16 * 2)
            for sm_ in (w_lo, rot, sT_cp, s_upd, t_vec, oT_lo, m_part, mT_lo, x2_add, n2_h, log_add, hT_lo):
                vec.sem_inc(sm_, SEED)
            vec.tensor_scalar(gmix[:], gmix[:], float(D) ** 0.5, None, ALU.mult).then_inc(g_scaled, 1)
            vec.wait_ge(g_scaled, 1)
            vec.memset(keep[:], 0.0).then_inc(vec_step, 1)
            vec.memset(glrT[:], 1.0).then_inc(ones_set, 1)
            vec.memset(logits[:, :, 36:40], -BIG).then_inc(vec_step, 1)
            vec.wait_ge(vec_step, 2)
            for j in range(TPS):
                norm1(j, 0)
            for j in range(TPS):
                hT_lo_part(j, 0)
            for w in (0, 1):
                for _ in split_lo(w, 0):
                    pass
            vec.wait_ge(par_in, 16 * 6)
            vec.tensor_scalar(ggla[:], ggla[:], float(HV) ** 0.5, None, ALU.mult).then_inc(g_scaled, 1)
            vec.tensor_scalar(gffn[:], gffn[:], float(D) ** 0.5, None, ALU.mult).then_inc(g_scaled, 1)
            vec.wait_ge(g_scaled, 3)
            with vec.Fori(0, SUPER) as s:
                vec.sem_clear(vec_step)
                step[0] = 0
                splits = split_lo(W_HEAD + 1, s)
                next(splits)
                for i in range(ITEMS + 5):
                    if i < ITEMS:
                        h, j = i // TPS, i % TPS
                        if i < RET_ITEMS:
                            vec.wait_ge(p_cp, tot(s, ITEMS, i + 1))
                            vec.wait_ge(tr_u, s * ITEMS + (SEED + i - 1))
                            x4 = pS[:, i % 4, 0:2 * HK].rearrange("p (a b c) -> p a b c", a=2, b=2)
                            rtab = cst[:, bass.ds(s * (TPS * ROT) + (C_ROT + j * ROT), ROT)]
                            cos = rtab[:, 0:32]
                            qk4 = qk[:, i % 2, :].rearrange("p (a b c) -> p a b c", a=2, b=2)
                            rt4 = rt[:].rearrange("p (a b c) -> p a b c", a=2, b=2)
                            mark(vec.tensor_tensor(qk4, x4, cos.unsqueeze(1).unsqueeze(1).to_broadcast([P, 2, 2, 32]), ALU.mult))
                            vec.wait_ge(rot, s * RET_ITEMS + (SEED + i))
                            for b in range(2):
                                sn = rtab[:, 32 + 32 * b:64 + 32 * b]
                                a_ = mark(vec.tensor_tensor(rt4[:, :, b, :], x4[:, :, 1 - b, :],
                                                            sn.unsqueeze(1).to_broadcast([P, 2, 32]), ALU.mult))
                            vec.wait_ge(vec_step, a_)
                            vec.tensor_tensor(qk[:, i % 2, :], qk[:, i % 2, :], rt[:], ALU.add).then_inc(rot, 1)
                        else:
                            vec.wait_ge(p_cp, tot(s, ITEMS, i + 1))
                            vec.wait_ge(tr_u, s * ITEMS + (SEED + i - 1))
                            vec.wait_ge(dec_e, s * 3 + (SEED + 3))
                            if i == RET_ITEMS:
                                vec.wait_ge(kd_done, tot(s, ITEMS, i))
                            hh = (h - HEADS) * HK
                            for c in range(2):
                                r = slice(c * CHUNK, (c + 1) * CHUNK)
                                ins = vec.tensor_tensor(kd[r, i % 2, c, :], pS[r, i % 4, HK:2 * HK],
                                                        edec[r, j, hh:hh + HK], ALU.mult)
                            ins.then_inc(kd_done, 1)
                    if 1 <= i <= ITEMS:
                        k = i - 1
                        h, j = k // TPS, k % TPS
                        vec.wait_ge(tr_u, tot(s, ITEMS, k + 1))
                        vec.wait_ge(o_mm, s * ITEMS + (SEED + k - (1 if j == TPS - 1 else 2)))
                        if h >= HEADS:
                            vec.wait_ge(dec_e, s * 3 + (SEED + 3))
                        cur = S0[:, h, :] if j == 0 else SW[:, (k - 1) % 4, 1, :]
                        for c in range(2):
                            u = ps[0:HK, B_U, c * HV:(c + 1) * HV]
                            if j == 0 and c == 0:
                                if h % HEADS == 0:
                                    vec.wait_ge(raw_st, s * 32 + (16 + h // HEADS * 16))
                                nxt = RAW[:, h % HEADS, :]
                            elif c == 0:
                                nxt = SW[:, k % 4, 0, :]
                            elif j == TPS - 1:
                                nxt = S0[:, h, :]
                            else:
                                nxt = SW[:, k % 4, 1, :]
                            if h < HEADS:
                                dec = float(np.exp(CHUNK * np.log1p(-np.exp2(-5.0 - h))))
                            else:
                                dec = aT[:, h - HEADS, 2 * j + c:2 * j + c + 1]
                            if c == 0 and j > 0:
                                vec.wait_ge(s_upd, s * ITEMS + (SEED + k))
                            ins = vec.scalar_tensor_tensor(nxt, cur, dec, u, ALU.mult, ALU.add)
                            if c == 1:
                                ins.then_inc(s_upd, 1)
                                break
                            vec.wait_ge(vec_step, mark(ins))
                            cur = nxt
                            if j == 0:
                                nxt = SW[:, k % 4, 0, :]
                                vec.wait_ge(vec_step, mark(vec.tensor_scalar(nxt, cur, keep[:], None, ALU.mult)))
                                cur = nxt
                    if 2 <= i <= RET_ITEMS + 1:
                        k = i - 2
                        vec.wait_ge(score, s * RET_ITEMS + (SEED + k + 1))
                        vec.wait_ge(o_mm, s * ITEMS + (SEED + k))
                        hh = k // TPS
                        vec.tensor_tensor(sT[:], ps[:, B_S, 0:P], cst3(C_DMAT + hh * P, P), ALU.mult)\
                           .then_inc(sT_cp, 1)
                    if 3 <= i <= ITEMS + 2:
                        k = i - 3
                        vec.wait_ge(o_mm, tot(s, ITEMS, k + 1))
                        vec.wait_ge(og_act, s * ITEMS + (SEED + k - 1))
                        if k < RET_ITEMS:
                            hh = k // TPS
                            vec.wait_ge(vec_step, mark(vec.tensor_scalar(
                                ob[:], ps[:, B_O, 0:HV], cst[:, C_QDEC + hh:C_QDEC + hh + 1], None, ALU.mult)))
                            vec.wait_ge(vec_step, mark(vec.tensor_tensor(ob[:], ob[:], ps[:, B_O, HV:2 * HV], ALU.add)))
                            a_ = mark(vec.bn_stats(st6[:, k % 2, :], ob[:]))
                            vec.wait_ge(vec_step, a_)
                            vec.wait_ge(rstd, s * ITEMS + (SEED + k - 1))
                            vec.bn_aggr(mv[:, k % 2, :], st6[:, k % 2, :]).then_inc(stat, 1)
                            vec.wait_ge(stat, s * ITEMS + (k + 1))
                            vec.wait_ge(silu, tot(s, ITEMS, k + 1))
                            vec.scalar_tensor_tensor(tb[:, k % 2, :], ob[:], mv[:, k % 2, 0:1], pS[:, k % 4, G],
                                                     ALU.subtract, ALU.mult).then_inc(t_vec, 1)
                        else:
                            vec.wait_ge(sgn_pool, s * (ITEMS - RET_ITEMS) + (SEED + k - RET_ITEMS + 1))
                            vec.wait_ge(stat, s * ITEMS + (k + 1))
                            vec.tensor_tensor(tb[:, k % 2, :], ps[:, B_O, 0:HV], pS[:, k % 4, G], ALU.mult)\
                               .then_inc(t_vec, 1)
                    if i >= 5:
                        k = i - 5
                        vec.wait_ge(oT_hi, tot(s, ITEMS, k + 1))
                        o = (slice(None), k // TPS, slice((k % TPS) * P, (k % TPS + 1) * P))
                        vec.tensor_tensor(oT[1][o], ps[:, B_OT, 0:P], oT[0][o].bitcast(F32), ALU.subtract)\
                           .then_inc(oT_lo, 1)
                    if i == 3:
                        laf, gaf = (x[:, :, :].rearrange("p t n -> p (t n)") for x in (la, ga))
                        vec.wait_ge(gate_l, s * 3 + (SEED + 3))
                        vec.wait_ge(vec_step, mark(vec.tensor_scalar(laf, laf, 0.0, None, ALU.min)))
                        vec.wait_ge(vec_step, mark(vec.tensor_tensor(laf, laf, gaf, ALU.subtract)))
                        vec.tensor_scalar(laf, laf, 1.0 / 16.0, None, ALU.mult).then_inc(gate_la, 1)
                    if i % TPS == TPS - 1 and i + 1 < ITEMS:
                        splits = split_lo(W_HEAD + (i + 1) // TPS + 1, s)
                    next(splits, None)
                vec.memset(keep[:], 1.0).then_inc(vec_step, 1)
                step[0] += 1
                def m_parts(d):
                    b0 = [(0, 1, 6, 7), (2, 3, 4, 5)][d % 2]
                    vec.wait_ge(z_sig, tot(s, DC, d + 1))
                    vec.wait_ge(br_mm, s * DC + (d + 1))
                    vec.wait_ge(m_sum, s * DC + (SEED + d))
                    mark(vec.tensor_tensor(mz[:, 0, :], sz[:, 0, :], ps[:, b0[2], 0:TOK], ALU.mult))
                    vec.tensor_tensor(mz[:, 1, :], sz[:, 1, :], ps[:, b0[3], 0:TOK], ALU.mult).then_inc(m_part, 1)

                def mt_low(d):
                    vec.wait_ge(mT_hi, tot(s, DC, d + 1))
                    vec.tensor_tensor(mT[1][:, d, :], mz[:, 2, :], mT[0][:, d, :].bitcast(F32), ALU.subtract)\
                       .then_inc(mT_lo, 1)

                for d in range(DC):
                    if d:
                        m_parts(d - 1)
                    for _ in split_lo(W_Z + d + 1, s):
                        pass
                    if d:
                        mt_low(d - 1)
                m_parts(DC - 1)
                mt_low(DC - 1)
                for n, (c0, cn) in enumerate(OUT_COLS):
                    if n < 2:
                        for _ in split_lo(W_OUT + n + 1, s):
                            pass
                    for j in range(TPS):
                        vec.wait_ge(out_mm, s * 3 * TPS + (SEED + n * TPS + j + 1))
                        vec.wait_ge(xr_in[j], s * 16 + 16)
                        vec.tensor_tensor(XR[j][:, c0:c0 + cn], XR[j][:, c0:c0 + cn],
                                          ps[:, (n * TPS + j) % 2, 0:cn], ALU.add).then_inc(x2_add, 1)
                    if n == 1:
                        for j in range(TPS):
                            norm1(j, s + 1)
                for _ in split_lo(0, s + 1):
                    pass
                for j in range(TPS):
                    hT_lo_part(j, s + 1)
                    vec.wait_ge(n2_rstd, tot(s, TPS, j + 1))
                    vec.wait_ge(n1_tr, s * TPS + (SEED + TPS + j + 1))
                    vec.wait_ge(x2_add, s * 3 * TPS + (SEED + 2 * TPS + j + 1))
                    vec.scalar_tensor_tensor(H[j][:], XR[j][:], rn[:, 3 + j:4 + j], gffn[:], ALU.mult, ALU.mult)\
                       .then_inc(n2_h, 1)
                for _ in split_lo(1, s + 1):
                    pass
                for j in range(TPS):
                    vec.wait_ge(log_mm, tot(s, TPS, j + 1))
                    vec.tensor_tensor(logits[:, bass.ds(s * TPS + j, 1), 0:36].rearrange("p o n -> p (o n)"),
                                      ps[:, j % 2, 0:36], rb[:], ALU.add).then_inc(log_add, 1)

        def z_banks(d):
            return [(0, 1, 6, 7), (2, 3, 4, 5)][d % 2]

        def z_part(pe, s, d, x, three, c0=0, c1=DC):
            w = W_Z + d
            if x == 0 and c0 == 0:
                pe.wait_ge(w_lo, s * NP_SB + (SEED + PIECE0[w] + PIECES[w]))
                if d == 0:
                    pe.wait_ge(p_cp, tot(s, ITEMS, ITEMS))
                elif d == 1:
                    pe.wait_ge(oT_lo, tot(s, ITEMS, ITEMS))
                else:
                    pe.wait_ge(m_part, s * DC + (SEED + d - 1))
            W = [whl[w % 2][i][:, x * PIECE:(x + 1) * PIECE].rearrange("p (c n) -> p c n", c=DC) for i in range(2)]
            A3 = slice(None)
            for c in range(c0, c1):
                ins = three(ps[:, z_banks(d)[x], 0:TOK], W, hT, (A3, c, A3), (A3, c, A3), c == 0, c == DC - 1)
            if c1 == DC:
                ins.then_inc(zr_mm, 1)

        def br_part(pe, s, d, three):
            w = W_Z + d
            if d == 0:
                pe.wait_ge(oT_lo, tot(s, ITEMS, ITEMS))
                pe.wait_ge(dec_e, s * 3 + (SEED + 3))
            A3 = slice(None)
            W = [whl[w % 2][i][:, 2 * PIECE:3 * PIECE].rearrange("p (c n) -> p c n", c=DC) for i in range(2)]
            for x in range(2):
                for c in range(HEADS):
                    ins = three(ps[:, z_banks(d)[2 + x], 0:TOK], W, oT, (A3, x * HEADS + c, A3), (A3, x * HEADS + c, A3),
                                c == 0, c == HEADS - 1)
            ins.then_inc(br_mm, 1)

        @block.tensor
        def _(pe):
            def three(out, A, B, ka, kb, start, stop):
                pe.matmul(out, A[0][ka], B[0][kb], start=start, stop=False)
                pe.matmul(out, A[0][ka], B[1][kb], start=False, stop=False)
                return pe.matmul(out, A[1][ka], B[0][kb], start=False, stop=stop)

            def transposes(j, src_):
                for c in range(DC):
                    ins = pe.transpose(ps[:, GB[j] + c // 4, (c % 4) * P:(c % 4 + 1) * P],
                                       src_[:, c * P:(c + 1) * P], ident)
                return ins

            A3 = slice(None)
            pe.wait_ge(cst_in, 16 * 2)
            for sm_ in (tr_u, o_mm, o_tr, n1_tr, n2_tr, log_mm, proj, zr_mm, glr_mm, gate_mm, dec_mm, out_mm, score):
                pe.sem_inc(sm_, SEED)
            for sm_ in (*x2_st, *h2_st, raw_st):
                pe.sem_inc(sm_, 16)
            for j in range(TPS):
                pe.wait_ge(n1_h, j + 1)
                transposes(j, H[j]).then_inc(n1_tr, 1)
            pe.wait_ge(par_in, 16 * 6)
            with pe.Fori(0, SUPER) as s:
                pe.wait_ge(hT_lo, s * (2 * TPS) + (SEED + 2 * TPS))
                pe.wait_ge(w_lo, s * NP_SB + (SEED + 1))
                pe.wait_ge(log_add, s * TPS + SEED)
                W = [whl[0][i][:, 0:PIECE].rearrange("p (c n) -> p c n", c=DC) for i in range(2)]
                for c in range(DC):
                    ins = three(ps[:, B_G, 0:TOK], W, hT, (A3, c, A3), (A3, c, A3),
                                c == 0, c == DC - 1)
                ins.then_inc(glr_mm, 1)
                for i in range(ITEMS + 5):
                    if i < ITEMS:
                        h, j = i // TPS, i % TPS
                        w = W_HEAD + h
                        if j == 0:
                            pe.wait_ge(w_lo, s * NP_SB + (SEED + PIECE0[w] + PIECES[w]))
                        pe.wait_ge(p_cp, s * ITEMS + (SEED + i - 1))
                        W = [whl[w % 2][x][:].rearrange("p (c n) -> p c n", c=DC) for x in range(2)]
                        for c in range(DC):
                            ins = three(ps[:, i % 2, 0:HW], hT, W, (A3, c, slice(j * P, (j + 1) * P)), (A3, c, A3),
                                        c == 0, c == DC - 1)
                        ins.then_inc(proj, 1)
                    elif i < ITEMS + 4:
                        x, half_ = divmod(i - ITEMS, 2)
                        z_part(pe, s, 0, x, three, half_ * DC // 2, (half_ + 1) * DC // 2)
                    if 1 <= i <= ITEMS:
                        k = i - 1
                        pe.wait_ge(p_cp, tot(s, ITEMS, k + 1))
                        pe.wait_ge(kd_done, tot(s, ITEMS, k + 1))
                        pe.wait_ge(qkT_cp, s * ITEMS + (SEED + k))
                        pe.wait_ge(s_upd, s * ITEMS + (SEED + k))
                        for c in range(2):
                            pe.matmul(ps[0:HK, B_U, c * HV:(c + 1) * HV], kd[:, k % 2, c, :], pS[:, k % 4, V],
                                      start=True, stop=True)
                        for x in range(2 if k < RET_ITEMS else 1):
                            ins = pe.transpose(ps[0:HK, B_T, x * P:(x + 1) * P],
                                               qk[:, k % 2, x * HK:(x + 1) * HK] if k < RET_ITEMS else pS[:, k % 4, 0:HK],
                                               ident)
                        ins.then_inc(tr_u, 1)
                    if 2 <= i <= RET_ITEMS + 1:
                        k = i - 2
                        pe.wait_ge(qkT_cp, tot(s, ITEMS, k + 1))
                        pe.wait_ge(sT_cp, s * RET_ITEMS + (SEED + k))
                        pe.matmul(ps[:, B_S, 0:P], qT(k, P, 2 * P), qT(k, 0, P), start=True, stop=True).then_inc(score, 1)
                    if 3 <= i <= ITEMS + 2:
                        k = i - 3
                        h, j = k // TPS, k % TPS
                        pe.wait_ge(t_vec, s * ITEMS + (SEED + k))
                        pe.wait_ge(qkT_cp, tot(s, ITEMS, k + 1))
                        pe.wait_ge(s_upd, tot(s, ITEMS, k + 1))
                        if k < RET_ITEMS:
                            pe.wait_ge(sT_cp, tot(s, RET_ITEMS, k + 1))
                            pe.matmul(ps[:, B_O, HV:2 * HV], sT[:], pS[:, k % 4, V], start=True, stop=True)
                        else:
                            pe.sem_inc(pe_seen, 1)
                        for c in range(2):
                            if k < RET_ITEMS:
                                st = SW[:, k % 4, 0, :] if c else (S0[:, h, :] if j == 0 else SW[:, (k - 1) % 4, 1, :])
                            elif c == 0:
                                st = RAW[:, h % HEADS, :] if j == 0 else SW[:, k % 4, 0, :]
                            else:
                                st = S0[:, h, :] if j == TPS - 1 else SW[:, k % 4, 1, :]
                            ins = pe.matmul(ps[c * CHUNK:(c + 1) * CHUNK, B_O, 0:HV],
                                            qT(k, c * CHUNK, (c + 1) * CHUNK), st, start=True, stop=True)
                        ins.then_inc(o_mm, 1)
                    if i >= 5:
                        k = i - 5
                        pe.wait_ge(og_act, tot(s, ITEMS, k + 1))
                        pe.wait_ge(oT_lo, s * ITEMS + (SEED + k))
                        pe.transpose(ps[:, B_OT, 0:P], og[:, k % 2, :], ident).then_inc(o_tr, 1)
                    if i in (1, 2):
                        if i == 1:
                            pe.wait_ge(glr_cp, s + 1)
                            pe.wait_ge(ones_set, 1)
                        else:
                            pe.wait_ge(gate_cp, s * 2 + (SEED + 1))
                        for j in ((0, 1), (2,))[i - 1]:
                            ins = pe.matmul(ps[:, B_G, (j % 2) * 256:(j % 2 + 1) * 256],
                                            glrT[0:RANK + 1, j * P:(j + 1) * P], gk2s[:], start=True, stop=True)
                        ins.then_inc(gate_mm, 1)
                    if i in (5, 6):
                        if i == 5:
                            pe.wait_ge(gate_la, s + 1)
                        else:
                            pe.wait_ge(dec_e, s * 3 + (SEED + 1))
                        for j in ((0, 1), (2,))[i - 5]:
                            ins = pe.matmul(ps[:, B_G, (j % 2) * 256:(j % 2 + 1) * 256], cst3(C_TRI, P), la[:, j, :],
                                            start=True, stop=True)
                        if i == 6:
                            for hh in range(HEADS):
                                for j in range(TPS):
                                    o = 256 + hh * 2 * TPS + 2 * j
                                    ins = pe.matmul(ps[0:HK, B_G, o:o + 2], la[:, j, hh * HK:(hh + 1) * HK], cst3(C_IND, 2),
                                                    start=True, stop=True)
                        ins.then_inc(dec_mm, 1)
                for d in range(DC):
                    for x in range(0 if d else 2, 2):
                        z_part(pe, s, d, x, three)
                    br_part(pe, s, d, three)
                for n, (c0, cn) in enumerate(OUT_COLS):
                    w = W_OUT + n
                    pe.wait_ge(w_lo, s * NP_SB + (SEED + PIECE0[w] + PIECES[w]))
                    W = [whl[w % 2][x][:, 0:DC * cn].rearrange("p (c n) -> p c n", c=DC) for x in range(2)]
                    def out_chunks(j, first, end):
                        for c in range(first, end):
                            ins = three(ps[:, (n * TPS + j) % 2, 0:cn], mT, W, (A3, c, slice(j * P, (j + 1) * P)),
                                        (A3, c, A3), c == 0, c == DC - 1)
                        return ins

                    if n == 0:
                        pe.wait_ge(mT_lo, tot(s, DC, DC - 1))
                        for j in range(2):
                            out_chunks(j, 0, DC - 1)
                        pe.wait_ge(mT_lo, tot(s, DC, DC))
                    for j in range(TPS):
                        o = n * TPS + j
                        if o >= 2:
                            pe.wait_ge(x2_add, s * 3 * TPS + (SEED + o - 1))
                        out_chunks(j, DC - 1 if o < 2 else 0, DC).then_inc(out_mm, 1)
                for j in range(TPS):
                    pe.wait_ge(n1_h, s * TPS + (TPS + j + 1))
                    transposes(j, H[j]).then_inc(n1_tr, 1)
                def router_transposes(j):
                    pe.wait_ge(n2_h, tot(s, TPS, j + 1))
                    pe.wait_ge(hT_lo, s * (2 * TPS) + (SEED + 2 * TPS + 2 * j + 2))
                    transposes(j, H[j]).then_inc(n2_tr, 1)

                def router_logits(j):
                    pe.wait_ge(n2_cp, s * TPS + (j + 1))
                    if j == 2:
                        pe.wait_ge(log_add, s * TPS + (SEED + 1))
                    for c in range(DC):
                        ins = pe.matmul(ps[:, j % 2, 0:36], h2T[:, j * D + c * P:j * D + (c + 1) * P], wr[:, c, :],
                                        start=(c == 0), stop=(c == DC - 1))
                    ins.then_inc(log_mm, 1)

                router_transposes(0)
                router_transposes(1)
                pe.wait_ge(x2_add, s * 3 * TPS + (SEED + 3 * TPS))
                router_logits(0)
                router_transposes(2)
                router_logits(1)
                router_logits(2)

        r_in = sem("r_in")
        r_vec = sem("r_vec")
        r_exp = sem("r_exp")
        r_ready = sem("r_ready")
        r_mm = sem("r_mm")
        l_st = sem("l_st")
        tix_in = sem("tix_in")
        pool_seen = sem("pool_seen")
        gx_in = sem("gx_in")
        gx_tr = sem("gx_tr")
        e_in = [sem(f"e_in{q}") for q in range(EP)]
        e_hi = [sem(f"e_hi{q}") for q in range(EP)]
        e_lo = [sem(f"e_lo{q}") for q in range(EP)]
        e_used = [sem(f"e_used{q}") for q in range(EP)]
        part.close()
        block2 = part.enter_context(nc.Block())

        def e_load(sp, b, q, first=False):
            e = sp.value_load(meta[0:1, bass.ds(b, 1)], min_val=0, max_val=EXPERTS - 1)
            rows = wexp[bass.ds(e, 1), q].rearrange("o p n -> p (o n)")
            if not first:
                sp.wait_ge(e_lo[q], b)
            sp.dma_start(est[q][:], rows).then_inc(e_in[q], 16)

        def e_split_hi(act, b, q, first=False):
            act.wait_ge(e_in[q], b * 16 + 16)
            if not first:
                act.wait_ge(e_used[q], b)
            act.activation(whi[q][:], est[q][:], ACT.Copy).then_inc(e_hi[q], 1)

        def e_split_lo(vec, b, q):
            vec.wait_ge(e_hi[q], b + 1)
            vec.tensor_tensor(wlo[q][:], est[q][:], whi[q][:].bitcast(F32), ALU.subtract).then_inc(e_lo[q], 1)

        def rows_of(pool, b, first=False):
            if not first:
                pool.wait_ge(gx_in, b * 16)
            pool.dma_start(tix[:], list_dram[bass.ds(b * TB, TB)]).then_inc(tix_in, 16)

        def gather(pool, b, first=False):
            pool.wait_ge(tix_in, b * 16 + 16)
            if not first:
                pool.wait_ge(gx_tr, b)
            pool.sem_inc(pool_seen, 1)
            pool.indirect_dma_start(out=gX[:], out_offset=None, in_=h2_dram,
                                    in_offset=bass.IndirectOffsetOnAxis(ap=tix[:, 0:1], axis=0)).then_inc(gx_in, 16)

        @block2.sync
        def _(sp):
            sp.wait_ge(r_ready, 6)
            for q in range(4):
                e_load(sp, 0, q, True)
            for j in range(TPS):
                sp.wait_ge(x2_st[j], 16 * (SUPER + 1))
                sp.wait_ge(h2_st[j], 16 * (SUPER + 1))
            sp.wait_ge(x2_pad, 16)
            sp.dma_start(gfin[:], g_final.partition_broadcast(P)).then_inc(r_in, 16)
            sp.wait_ge(r_in, 16)

        @block2.scalar
        def _(act):
            act.wait_ge(r_ready, 2)
            act.activation(gex[:], ngm[:], ACT.Exp).then_inc(r_exp, 1)
            act.activation(ex[:], dd[:], ACT.Exp).then_inc(r_exp, 1)
            for q in range(4):
                e_split_hi(act, 0, q, True)

        @block2.gpsimd
        def _(pool):
            pool.wait_ge(l_init, 16)
            pool.wait_ge(r_ready, 7)
            for t in range(TILES):
                for k in range(2):
                    pool.indirect_dma_start(out=list_dram, out_offset=bass.IndirectOffsetOnAxis(ap=dst[:, k, t:t + 1], axis=0),
                                            in_=tokid[:, t, k, :], in_offset=None).then_inc(l_st, 16)
            pool.wait_ge(l_st, 16 * 2 * TILES)
            for j in range(TPS):
                pool.wait_ge(x2_st[j], 16 * (SUPER + 1))
                pool.wait_ge(h2_st[j], 16 * (SUPER + 1))
            rows_of(pool, 0, True)
            gather(pool, 0, True)

        @block2.vector
        def _(vec):
            n = [0]

            def link(ins):
                n[0] += 1
                ins.then_inc(r_vec, 1)
                vec.wait_ge(r_vec, n[0])

            def mark(ins):
                n[0] += 1
                ins.then_inc(r_vec, 1)

            def by_tile(ap):
                return ap.unsqueeze(1).to_broadcast([P, TILES, EXPERTS])

            def by_expert(ap, e=EXPERTS):
                return ap.unsqueeze(2).to_broadcast([P, TILES, e])

            vec.memset(ones[:], 1.0).then_inc(r_ready, 1)
            mark(vec.memset(runs[:, 0, :], 0.0))
            for k in range(2):
                for c in range(2):
                    mark(vec.tensor_copy(tokid[:, :, k, c], cst3(C_TOKID, TILES)))
            for t in range(TILES):
                mark(vec.max(gm8[:, t, :], logits[:, t, 32:40]))
            vec.wait_ge(r_vec, n[0])
            for t in range(TILES):
                mark(vec.max_index(gi8[:, t, :], gm8[:, t, :], logits[:, t, 32:40]))
            vec.wait_ge(r_vec, n[0])
            link(vec.tensor_copy(gif[:], gi8[:, :, 0]))
            link(vec.tensor_tensor(gmask[:], by_tile(cst3(C_GRP, EXPERTS)), by_expert(gif[:]), ALU.is_equal))
            mark(vec.tensor_scalar(pen[:], gmask[:], BIG, -BIG, ALU.mult, ALU.add))
            link(vec.tensor_tensor(lm[:], logits[:, :, 0:EXPERTS], gmask[:], ALU.mult))
            link(vec.tensor_tensor(lm[:], lm[:], pen[:], ALU.add))
            for t in range(TILES):
                mark(vec.max(em8[:, t, :], lm[:, t, :]))
            vec.wait_ge(r_vec, n[0])
            for t in range(TILES):
                mark(vec.max_index(ei8[:, t, :], em8[:, t, :], lm[:, t, :]))
            vec.wait_ge(r_vec, n[0])
            mark(vec.tensor_tensor(ngm[:], logits[:, :, 32:36], by_expert(gm8[:, :, 0], GROUPS), ALU.subtract))
            vec.tensor_tensor(dd[:], em8[:, :, 1], em8[:, :, 0], ALU.subtract).then_inc(r_ready, 1)
            link(vec.tensor_copy(eif[:], ei8[:, :, 0:2]))
            for k in range(2):
                link(vec.tensor_tensor(oh[k][:], by_tile(cst3(C_IOTA, EXPERTS)), by_expert(eif[:, :, k]), ALU.is_equal))
                link(vec.tensor_tensor(oh[k][:], oh[k][:], by_expert(cst3(C_VALID, TILES)), ALU.mult))
            link(vec.tensor_tensor(both[:], oh[0][:], oh[1][:], ALU.add))
            for t in range(TILES):
                ins = vec.tensor_tensor(runs[:, t + 1, :], runs[:, t, :], both[:, t, :], ALU.add)
                if t < TILES - 1:
                    link(ins)
            ins.then_inc(r_ready, 1)
            vec.wait_ge(r_mm, 1)
            link(vec.tensor_copy(cntc[:], ps[0:EXPERTS, 1, 0:1]))
            link(vec.tensor_scalar(cmp[:], cst[0:EXPERTS, C_STEP:C_STEP + MAX_PER_EXPERT], cntc[:], None, ALU.is_lt))
            link(vec.tensor_reduce(nbc[:], cmp[:], AX.X, ALU.add))
            vec.tensor_scalar(nbb[:], ones[0:EXPERTS, :], nbc[:], None, ALU.mult).then_inc(r_ready, 1)
            vec.wait_ge(r_mm, 2)
            mark(vec.tensor_copy(pstart[:], ps[:, 2, 0:EXPERTS]))
            link(vec.tensor_copy(bend[:], ps[0:EXPERTS, 3, 0:1]))
            vec.tensor_scalar(bcmp[:], cst[0:EXPERTS, C_IOTAB:C_IOTAB + 64], bend[:], None, ALU.is_ge)\
               .then_inc(r_ready, 1)
            link(vec.tensor_tensor(rank[:], ps[:, 0, 0:TILES * EXPERTS].rearrange("p (t e) -> p t e", t=TILES),
                                   by_tile(pstart[:]), ALU.add))
            for k in range(2):
                link(vec.tensor_tensor(pick[:], oh[k][:], rank[:], ALU.mult))
                link(vec.tensor_reduce(dstf[:, k, :], pick[:], AX.X, ALU.add))

            link(vec.tensor_tensor(dstf[:], dstf[:], cst3(C_DUMP, 2 * TILES).rearrange("p (k t) -> p k t", k=2), ALU.add))
            vec.wait_ge(r_mm, 3)
            link(vec.tensor_scalar(metaf[:, 0:64], ps[0:1, 4, 0:64], float(EXPERTS - 1), None, ALU.min))
            link(vec.tensor_tensor(metaf[:, 64:72], ps[0:1, 5, 0:8], cst[0:1, C_IOTAB:C_IOTAB + 8], ALU.subtract))
            vec.tensor_copy(meta[:], metaf[:]).then_inc(r_ready, 1)
            mark(vec.tensor_copy(dst[:], dstf[:]))
            vec.wait_ge(r_exp, 2)
            mark(vec.tensor_reduce(gsum[:], gex[:], AX.X, ALU.add))
            link(vec.tensor_scalar(den[:], ex[:], 1.0, None, ALU.add))
            mark(vec.reciprocal(pg[:], gsum[:]))
            link(vec.reciprocal(g1[:], den[:]))
            link(vec.tensor_tensor(g1[:], g1[:], pg[:], ALU.mult))
            mark(vec.tensor_copy(tokid[:, :, 0, 2].bitcast(F32), g1[:]))
            link(vec.tensor_tensor(tokid[:, :, 1, 2].bitcast(F32), g1[:], ex[:], ALU.mult))
            vec.sem_inc(r_ready, 1)
            e_split_lo(vec, 0, 0)

        @block2.tensor
        def _(pe):
            pe.wait_ge(r_ready, 3)
            o = slice(0, TILES * EXPERTS)
            pe.matmul(ps[:, 0, o], cst3(C_LOW, P), both[:].rearrange("p t e -> p (t e)"), start=True, stop=False)
            pe.matmul(ps[:, 0, o], ones[:], runs[:, 0:TILES, :].rearrange("p t e -> p (t e)"), start=False, stop=True)
            pe.matmul(ps[0:EXPERTS, 1, 0:1], runs[:, TILES, :], ones[:, 0:1], start=True, stop=True).then_inc(r_mm, 1)
            pe.wait_ge(r_ready, 4)
            pe.matmul(ps[:, 2, 0:EXPERTS], nbb[:], cst[0:EXPERTS, C_TRI32:C_TRI32 + EXPERTS], start=True, stop=True)
            pe.matmul(ps[0:EXPERTS, 3, 0:1], cst[0:EXPERTS, C_TRI32I:C_TRI32I + EXPERTS], nbc[:], start=True, stop=True)\
              .then_inc(r_mm, 1)
            pe.wait_ge(r_ready, 5)
            pe.matmul(ps[0:1, 4, 0:64], ones[0:EXPERTS, 0:1], bcmp[:], start=True, stop=True)
            pe.matmul(ps[0:1, 5, 0:8], nbc[:], ones[0:EXPERTS, 0:8], start=True, stop=True).then_inc(r_mm, 1)

        pix_in = sem("pix_in")
        y_free = sem("y_free")
        xT_hi = sem("xT_hi")
        xT_lo = sem("xT_lo")
        e_silu = sem("e_silu")
        hid_v = sem("hid_v")
        hid_tr = sem("hid_tr")
        hidT_hi = sem("hidT_hi")
        hidT_lo = sem("hidT_lo")
        y_act = sem("y_act")
        y_vec = sem("y_vec")
        y_st = sem("y_st")
        part.close()
        block3 = part.enter_context(nc.Block())

        def blocks_of(eng, less=0):
            return eng.value_load(meta[0:1, 64 + less:65 + less], min_val=PAIRS // TB - less,
                                  max_val=MAX_BLOCKS - less)

        def body_pieces(b, last=False):
            ahead = [] if last else [(b + 1, q) for q in (1, 2, 3)]
            return ahead + [(b, 4), (b, 5)] + ([] if last else [(b + 2, 0)])

        @block3.sync
        def _(sp):
            last = blocks_of(sp, 1)

            for b, q in [(1, 0)] + body_pieces(0):
                e_load(sp, b, q, b == 0)
            with sp.Fori(1, last) as b:
                for c, q in body_pieces(b):
                    e_load(sp, c, q)
            for c, q in body_pieces(last, True):
                e_load(sp, c, q)

        @block3.gpsimd
        def _(pool):
            nb, last, second_last, third_last = (blocks_of(pool, n) for n in range(4))



            def pairs_of(b):
                pool.dma_start(pix[:], list_dram[bass.ds(b * TB, TB)]).then_inc(pix_in, 16)

            def scatter(b):
                pool.wait_ge(y_act, b + 1)
                pool.wait_ge(y_vec, b + 1)
                pool.sem_inc(pool_seen, 1)
                pool.indirect_dma_start(out=x2_dram, out_offset=bass.IndirectOffsetOnAxis(ap=pix[:, 1:2], axis=0),
                                        in_=yS[:], in_offset=None, compute_op=ALU.add).then_inc(y_st, 16)

            def stored(b):
                pool.wait_ge(y_st, b * 16 + 16)
                pool.sem_inc(y_free, 1)

            for b in range(1, 3):
                rows_of(pool, b)
                gather(pool, b)
            rows_of(pool, 3)
            with pool.Fori(0, third_last) as b:
                pairs_of(b)
                gather(pool, b + 3)
                scatter(b)
                rows_of(pool, b + 4)
                stored(b)
            for b in (third_last, second_last, last):
                pairs_of(b)
                scatter(b)
                stored(b)
            pool.wait_ge(tix_in, nb * 16 + 16)

        @block3.scalar
        def _(act):
            last = blocks_of(act, 1)

            def hi(b, q, first=False):
                e_split_hi(act, b, q, first)

            def x_hi(b, first=False):
                act.wait_ge(gx_tr, b + 1)
                if not first:
                    act.wait_ge(e_used[3], b)
                for g in range(2):
                    act.activation(xT[0][:, 4 * g:4 * g + 4, :],
                                   ps[:, 2 + g, 0:4 * TB].rearrange("p (c t) -> p c t", c=4), ACT.Copy).then_inc(xT_hi, 1)

            def y_out(b):
                act.wait_ge(e_used[5], b + 1)
                act.wait_ge(pix_in, b * 16 + 16)
                act.wait_ge(y_free, b + SEED)
                act.activation(yS[:, 0:512], ps[0:TB, 5, :], ACT.Copy, scale=pix[:, 2:3].bitcast(F32)).then_inc(y_act, 1)

            def body(b, first=False, last=False):
                act.wait_ge(e_used[1], b + 1)
                if not first:
                    act.wait_ge(hid_v, b)
                act.activation(sgate[:], ps[0:TB, 0, :], ACT.Silu).then_inc(e_silu, 1)
                if not last:
                    hi(b + 1, 1)
                    hi(b + 1, 2)
                    hi(b + 1, 3)
                    x_hi(b + 1)
                hi(b, 4, first)
                hi(b, 5, first)
                if not first:
                    y_out(b - 1)
                act.wait_ge(hid_tr, b + 1)
                act.activation(hidT[0][:], ps[:, 4, 0:EC * TB].rearrange("p (c t) -> p c t", c=EC), ACT.Copy)\
                   .then_inc(hidT_hi, 1)
                if not last:
                    hi(b + 2, 0)

            act.sem_inc(y_free, SEED)
            x_hi(0, True)
            hi(1, 0)
            body(0, first=True)
            with act.Fori(1, last) as b:
                body(b)
            body(last, last=True)
            y_out(last)

        @block3.vector
        def _(vec):
            last = blocks_of(vec, 1)

            def lo(b, q):
                e_split_lo(vec, b, q)

            def x_lo(b):
                for g in range(2):
                    vec.wait_ge(xT_hi, b * 2 + (g + 1))
                    vec.tensor_tensor(xT[1][:, 4 * g:4 * g + 4, :],
                                      ps[:, 2 + g, 0:4 * TB].rearrange("p (c t) -> p c t", c=4),
                                      xT[0][:, 4 * g:4 * g + 4, :].bitcast(F32), ALU.subtract).then_inc(xT_lo, 1)

            def y_out(b):
                vec.wait_ge(e_used[5], b + 1)
                vec.wait_ge(pix_in, b * 16 + 16)
                vec.wait_ge(y_free, b + SEED)
                vec.tensor_scalar(yS[:, 512:1024], ps[0:TB, 6, :], pix[:, 2:3].bitcast(F32), None, ALU.mult)\
                   .then_inc(y_vec, 1)

            def body(b, first=False, last=False):
                if not last:
                    lo(b + 1, 1)
                    lo(b + 1, 2)
                vec.wait_ge(e_silu, b + 1)
                vec.wait_ge(e_used[3], b + 1)
                if not first:
                    vec.wait_ge(hid_tr, b)
                vec.tensor_tensor(hid[:], sgate[:], ps[0:TB, 1, :], ALU.mult).then_inc(hid_v, 1)
                if not last:
                    lo(b + 1, 3)
                    x_lo(b + 1)
                lo(b, 4)
                lo(b, 5)
                if not first:
                    y_out(b - 1)
                vec.wait_ge(hidT_hi, b + 1)
                vec.tensor_tensor(hidT[1][:], ps[:, 4, 0:EC * TB].rearrange("p (c t) -> p c t", c=EC),
                                  hidT[0][:].bitcast(F32), ALU.subtract).then_inc(hidT_lo, 1)
                if not last:
                    lo(b + 2, 0)

            lo(0, 1)
            lo(0, 2)
            x_lo(0)
            lo(0, 3)
            lo(1, 0)
            body(0, first=True)
            with vec.Fori(1, last) as b:
                body(b)
            body(last, last=True)
            y_out(last)

        @block3.tensor
        def _(pe):
            last, second_last = blocks_of(pe, 1), blocks_of(pe, 2)

            def three(out, A, B, ka, kb, start, stop):
                pe.matmul(out, A[0][ka], B[0][kb], start=start, stop=False)
                pe.matmul(out, A[0][ka], B[1][kb], start=False, stop=False)
                return pe.matmul(out, A[1][ka], B[0][kb], start=False, stop=stop)

            A3 = slice(None)

            def x_transposes(b, first=False):
                pe.wait_ge(gx_in, b * 16 + 16)
                if not first:
                    pe.wait_ge(xT_lo, b * 2)
                for c in range(DC):
                    ins = pe.transpose(ps[:, 2 + c // 4, (c % 4) * TB:(c % 4 + 1) * TB], gX[:, c * P:(c + 1) * P],
                                       ident[0:TB, 0:TB])
                ins.then_inc(gx_tr, 1)

            def gate_up(b, first):
                pe.wait_ge(xT_lo, b * 2 + 2)
                for m, bank_read in ((0, e_silu), (1, hid_v)):
                    if not first:
                        pe.wait_ge(bank_read, b)
                    for h in range(2):
                        q = 2 * m + h
                        pe.wait_ge(e_lo[q], b + 1)
                        W = [w[q][:].rearrange("p (c n) -> p c n", n=DE) for w in (whi, wlo)]
                        for c in range(4):
                            ins = three(ps[0:TB, m, :], xT, W, (A3, 4 * h + c, A3), (A3, c, A3),
                                        h == 0 and c == 0, h == 1 and c == 3)
                        ins.then_inc(e_used[q], 1)

            def down(b, first=False):
                pe.wait_ge(hidT_lo, b + 1)
                if not first:
                    pe.wait_ge(y_act, b)
                    pe.wait_ge(y_vec, b)
                for h in range(2):
                    pe.wait_ge(e_lo[4 + h], b + 1)
                    W = [w[4 + h][:].rearrange("p (c n) -> p c n", n=D) for w in (whi, wlo)]
                    for c in range(2):
                        for n in range(2):
                            ins = three(ps[0:TB, 5 + n, :], hidT, W, (A3, 2 * h + c, A3),
                                        (A3, c, slice(n * 512, (n + 1) * 512)),
                                        h == 0 and c == 0, h == 1 and c == 1)
                    ins.then_inc(e_used[4 + h], 1)

            def hid_transposes(b, first=False):
                pe.wait_ge(hid_v, b + 1)
                if not first:
                    pe.wait_ge(hidT_lo, b)
                for c in range(EC):
                    ins = pe.transpose(ps[:, 4, c * TB:(c + 1) * TB], hid[:, c * P:(c + 1) * P], ident[0:TB, 0:TB])
                ins.then_inc(hid_tr, 1)

            x_transposes(0, True)
            gate_up(0, True)
            x_transposes(1)
            hid_transposes(0, True)
            gate_up(1, False)
            x_transposes(2)
            down(0, True)
            hid_transposes(1)
            with pe.Fori(1, second_last) as b:
                gate_up(b + 1, False)
                x_transposes(b + 2)
                down(b)
                hid_transposes(b + 1)
            gate_up(last, False)
            down(second_last)
            hid_transposes(last)
            down(last)

        c_x = [sem(f"c_x{t}") for t in range(TILES)]
        c_sum = sem("c_sum")
        c_pool = sem("c_pool")
        c_rstd = sem("c_rstd")
        c_out = sem("c_out")
        c_st = sem("c_st")
        part.close()
        block4 = part.enter_context(nc.Block())

        @block4.sync
        def _(sp):
            for t in range(TILES):
                sp.dma_start(cx[t][:], x2_dram[t * P:(t + 1) * P]).then_inc(c_x[t], 16)

        @block4.gpsimd
        def _(pool):
            for t in range(TILES):
                pool.wait_ge(c_sum, t + 1)
                pool.tensor_tensor(cq[:, TILES + t:TILES + t + 1], cq[:, t:t + 1], half[:, 3:4], ALU.add)\
                    .then_inc(c_pool, 1)
                pool.wait_ge(c_pool, t + 1)
                pool.tensor_tensor(cq[:, 2 * TILES + t:2 * TILES + t + 1], cq[:, TILES + t:TILES + t + 1], half[:, 0:1],
                                   ALU.pow).then_inc(c_rstd, 1)

        @block4.scalar
        def _(act):
            def store(t):
                act.wait_ge(c_out, t + 1)
                act.dma_start(y_all[t], co[t][:]).then_inc(c_st, 16)

            for t in range(TILES):
                act.wait_ge(c_x[t], 16)
                if t:
                    act.wait_ge(c_sum, t)
                act.activation(cscr[:], cx[t][:], ACT.Square, accum_out=cq[:, t:t + 1]).then_inc(c_sum, 1)
                if t >= 2:
                    store(t - 2)
            store(TILES - 2)
            store(TILES - 1)
            act.wait_ge(c_st, 16 * TILES)

        @block4.vector
        def _(vec):
            vec.tensor_scalar(gfin[:], gfin[:], float(D) ** 0.5, None, ALU.mult).then_inc(g_scaled, 1)
            vec.wait_ge(g_scaled, 4)
            for t in range(TILES):
                vec.wait_ge(c_x[t], 16)
                vec.wait_ge(c_rstd, t + 1)
                vec.scalar_tensor_tensor(co[t][:], cx[t][:], cq[:, 2 * TILES + t:2 * TILES + t + 1], gfin[:],
                                         ALU.mult, ALU.mult).then_inc(c_out, 1)

        part.close()


def lay_out(x_prompt, x_sample, state_ret, state_gla, meta_tokens, g_mix, w_in, w_gla_gk2, b_gla_gk, g_gla_norm,
            w_br_ret, w_br_gla, w_out, g_ffn, w_router_group, b_router_group, w_router_expert, b_router_expert,
            w_exp_gate, w_exp_up, w_exp_down, g_final):
    f = np.float32
    x_all = np.zeros((TILES + TPS, P, D), f)
    rows = x_all.reshape(-1, D)
    rows[0:DEC_SEQ] = x_sample[0]
    rows[FIRST_META:FIRST_META + N_META] = meta_tokens
    rows[DEC_SEQ + CHUNK:ROWS] = x_prompt[0]
    states = np.concatenate([state_ret[0, 0], state_gla[0, 0]]).transpose(1, 0, 2)
    RK, RV = HEADS * HK, HEADS * HV
    cuts = np.cumsum([0, RK, RK, RV, RV, RK, RK, RV, RV, RANK, D, D])
    w = w_in[0]
    part = [w[:, cuts[i]:cuts[i + 1]] for i in range(11)]

    def chunked(m):
        return m.reshape(-1, P, m.shape[1]).transpose(1, 0, 2).reshape(P, -1)

    def pieces(m):
        return list(m.reshape(P, -1, PIECE).transpose(1, 0, 2))

    low = np.zeros((D, P), f)
    low[:, 0:RANK] = part[8]
    out = pieces(chunked(low))
    for h in range(NHB):
        q, k, v, g = part[0:4] if h < HEADS else part[4:8]
        i = h % HEADS
        out += pieces(chunked(np.concatenate([q[:, i * HK:(i + 1) * HK], k[:, i * HK:(i + 1) * HK],
                                              v[:, i * HV:(i + 1) * HV], g[:, i * HV:(i + 1) * HV]], axis=1)))
    for d in range(DC):
        c = slice(d * P, (d + 1) * P)
        out += pieces(np.concatenate([chunked(part[9][:, c]), chunked(part[10][:, c]), chunked(w_br_ret[0][:, c]),
                                      chunked(w_br_gla[0][:, c])], axis=1))
    for c0, cn in OUT_COLS:
        out += pieces(chunked(w_out[0][:, c0:c0 + cn]))
    wmix = np.stack(out)
    E_ = EXPERTS
    gu = [x[0].reshape(E_, 2, 4, P, DE).transpose(0, 1, 3, 2, 4).reshape(E_, 2, P, EPC) for x in (w_exp_gate, w_exp_up)]
    dn = w_exp_down[0].reshape(E_, 2, 2, P, D).transpose(0, 1, 3, 2, 4).reshape(E_, 2, P, EPC)
    return {
        "x_all": x_all, "states": states, "consts": shape_constants(), "list_init": empty_list(), "g_mix": g_mix[0], "g_ffn": g_ffn[0],
        "g_final": g_final, "g_gla": g_gla_norm[0], "wmix": wmix,
        "gk2": np.concatenate([w_gla_gk2[0], b_gla_gk[0][None]]),
        "w_router": np.concatenate([w_router_expert[0], w_router_group[0]], axis=1).reshape(DC, P, 36).transpose(1, 0, 2),
        "b_router": np.concatenate([b_router_expert[0], b_router_group[0]]),
        "wexp": np.concatenate(gu + [dn], axis=1),
    }


OUTS = {"y_all": (TILES, P, D), "raw_out": (2 * SUPER, HK, HEADS, HV), "fin_out": (HK, NHB, HV)}


def kernel(**inputs):
    import concourse.bacc as bacc
    from concourse.bass_utils import run_bass_kernel_spmd

    arrays = {n: np.ascontiguousarray(a) for n, a in lay_out(**{n: np.asarray(a) for n, a in inputs.items()}).items()}
    nc = bacc.Bacc("TRN2", target_bir_lowering=False, num_devices=1)
    args = [nc.dram_tensor(n, a.shape, mybir.dt.from_np(a.dtype), kind="ExternalInput").ap() for n, a in arrays.items()]
    args += [nc.dram_tensor(n, s, F32, kind="ExternalOutput").ap() for n, s in OUTS.items()]
    build(nc, *args)
    got = run_bass_kernel_spmd(nc, [arrays], core_ids=[0]).results[0]
    y = np.asarray(got["y_all"]).reshape(ROWS, D)
    raw = np.asarray(got["raw_out"])[0:2].transpose(0, 2, 1, 3)
    fin = np.asarray(got["fin_out"]).transpose(1, 0, 2)

    def state(a):
        return np.ascontiguousarray(a)[None, None]

    return (y[None, DEC_SEQ + CHUNK:], y[None, 0:DEC_SEQ], state(fin[:HEADS]), state(fin[HEADS:]),
            state(raw[0]), state(raw[1]))
```
